# Optimizing a Trainium2 kernel written in Bass

```python
import jax, jax.numpy as jnp
from jax import lax
import numpy as np

D_MODEL = 1024
BATCH = 1
SEQ = 1024
DEPTH = 1

MEM_LEN = 256
HEAD_DIM = 64
SB_HEADS = 8
FOX_HEADS = 8
MEM_HEADS = 4
SB_WIDTH = SB_HEADS * HEAD_DIM
FOX_WIDTH = FOX_HEADS * HEAD_DIM
MEM_WIDTH = MEM_HEADS * HEAD_DIM
MIX_WIDTH = SB_WIDTH + FOX_WIDTH + MEM_WIDTH
TOTAL_HEADS = SB_HEADS + FOX_HEADS + MEM_HEADS
IN_WIDTH = 3 * SB_WIDTH + 3 * FOX_WIDTH + FOX_HEADS + MEM_WIDTH + MIX_WIDTH
Q_BLOCK = 128
EPS = 1e-6

kernel_name = "hybrid_stickbreak_fox_memxattn"

def rmsnorm(x, g):
    xf = x.astype(jnp.float32)
    y = xf * lax.rsqrt(jnp.mean(xf * xf, axis=-1, keepdims=True) + EPS)
    return (y * g.astype(jnp.float32)).astype(x.dtype)

def split_heads(t, n_heads):
    b, s, _ = t.shape
    return t.reshape(b, s, n_heads, HEAD_DIM).transpose(0, 2, 1, 3)

def merge_heads(t):
    b, h, s, d = t.shape
    return t.transpose(0, 2, 1, 3).reshape(b, s, h * d)

def stick_breaking_attention(q, k, v):
    seq = q.shape[2]
    scale = HEAD_DIM ** -0.5
    outs = []
    for i in range(seq // Q_BLOCK):
        start, end = i * Q_BLOCK, (i + 1) * Q_BLOCK
        qb, kb, vb = q[:, :, start:end], k[:, :, :end], v[:, :, :end]
        z = jnp.einsum('bhqd,bhkd->bhqk', qb, kb,
                       preferred_element_type=jnp.float32) * scale
        q_pos = start + jnp.arange(Q_BLOCK)[:, None]
        k_pos = jnp.arange(end)[None, :]
        strict = k_pos < q_pos
        log_fail = jnp.where(strict, -jax.nn.softplus(z), 0.0)
        suffix = lax.cumsum(log_fail, axis=3, reverse=True) - log_fail
        log_a = jax.nn.log_sigmoid(z) + suffix
        a = jnp.where(strict, jnp.exp(log_a), 0.0)
        outs.append(jnp.einsum('bhqk,bhkd->bhqd', a.astype(vb.dtype), vb))
    return jnp.concatenate(outs, axis=2)

def forgetting_attention(q, k, v, log_f_cum):
    seq = q.shape[2]
    scale = HEAD_DIM ** -0.5
    outs = []
    for i in range(seq // Q_BLOCK):
        start, end = i * Q_BLOCK, (i + 1) * Q_BLOCK
        qb, kb, vb = q[:, :, start:end], k[:, :, :end], v[:, :, :end]
        logits = jnp.einsum('bhqd,bhkd->bhqk', qb, kb,
                            preferred_element_type=jnp.float32) * scale
        logits = logits + log_f_cum[:, :, start:end, None] - log_f_cum[:, :, None, :end]
        q_pos = start + jnp.arange(Q_BLOCK)[:, None]
        k_pos = jnp.arange(end)[None, :]
        logits = jnp.where(k_pos <= q_pos, logits, -jnp.inf)
        p = jax.nn.softmax(logits, axis=-1)
        outs.append(jnp.einsum('bhqk,bhkd->bhqd', p.astype(vb.dtype), vb))
    return jnp.concatenate(outs, axis=2)

def memory_attention(q, k, v):
    logits = jnp.einsum('bhqd,bhkd->bhqk', q, k,
                        preferred_element_type=jnp.float32) * (HEAD_DIM ** -0.5)
    p = jax.nn.softmax(logits, axis=-1)
    return jnp.einsum('bhqk,bhkd->bhqd', p.astype(v.dtype), v)

def setup_inputs(seed: int = 0) -> dict:
    key = jax.random.key(seed)
    ks = jax.random.split(key, 11)
    f32 = jnp.float32
    x = jax.random.normal(ks[0], (BATCH, SEQ, D_MODEL), f32)
    mem = jax.random.normal(ks[1], (BATCH, MEM_LEN, D_MODEL), f32)
    norm_w = 1.0 + 0.02 * jax.random.normal(ks[2], (DEPTH, D_MODEL), f32)
    w_in = jax.random.normal(ks[3], (DEPTH, D_MODEL, IN_WIDTH), f32) * D_MODEL ** -0.5
    b_forget = 0.1 * jax.random.normal(ks[4], (DEPTH, FOX_HEADS), f32)
    mem_norm_w = 1.0 + 0.02 * jax.random.normal(ks[5], (DEPTH, D_MODEL), f32)
    w_mem_kv = jax.random.normal(ks[6], (DEPTH, D_MODEL, 2 * MEM_WIDTH), f32) * D_MODEL ** -0.5
    out_norm_w = 1.0 + 0.02 * jax.random.normal(ks[7], (DEPTH, MIX_WIDTH), f32)
    w_out = jax.random.normal(ks[8], (DEPTH, MIX_WIDTH, D_MODEL), f32) * MIX_WIDTH ** -0.5
    final_norm_w = 1.0 + 0.02 * jax.random.normal(ks[9], (D_MODEL,), f32)
    return {"x": x, "mem": mem, "norm_w": norm_w, "w_in": w_in, "b_forget": b_forget,
            "mem_norm_w": mem_norm_w, "w_mem_kv": w_mem_kv, "out_norm_w": out_norm_w,
            "w_out": w_out, "final_norm_w": final_norm_w}

def reference(x, mem, norm_w, w_in, b_forget, mem_norm_w, w_mem_kv, out_norm_w, w_out,
              final_norm_w):
    sizes = [SB_WIDTH] * 3 + [FOX_WIDTH] * 3 + [FOX_HEADS, MEM_WIDTH, MIX_WIDTH]
    offsets = [int(o) for o in np.cumsum(sizes)[:-1]]
    b, s, _ = x.shape
    for layer in range(DEPTH):
        h = rmsnorm(x, norm_w[layer])
        proj = h @ w_in[layer]
        (sb_q, sb_k, sb_v, fx_q, fx_k, fx_v, f_logit, m_q, gate) = jnp.split(proj, offsets, axis=-1)

        sb_out = stick_breaking_attention(split_heads(sb_q, SB_HEADS), split_heads(sb_k, SB_HEADS),
                                          split_heads(sb_v, SB_HEADS))

        log_f = jax.nn.log_sigmoid((f_logit + b_forget[layer]).astype(jnp.float32))
        log_f_cum = jnp.cumsum(log_f.transpose(0, 2, 1), axis=-1)
        fx_out = forgetting_attention(split_heads(fx_q, FOX_HEADS), split_heads(fx_k, FOX_HEADS),
                                      split_heads(fx_v, FOX_HEADS), log_f_cum)

        mem_kv = rmsnorm(mem, mem_norm_w[layer]) @ w_mem_kv[layer]
        m_k, m_v = jnp.split(mem_kv, 2, axis=-1)
        m_out = memory_attention(split_heads(m_q, MEM_HEADS), split_heads(m_k, MEM_HEADS),
                                 split_heads(m_v, MEM_HEADS))

        y = jnp.concatenate([merge_heads(sb_out), merge_heads(fx_out), merge_heads(m_out)], axis=-1)
        yf = y.astype(jnp.float32).reshape(b, s, TOTAL_HEADS, HEAD_DIM)
        yf = yf * lax.rsqrt(jnp.mean(yf * yf, axis=-1, keepdims=True) + EPS)
        yf = yf.reshape(b, s, MIX_WIDTH) * out_norm_w[layer].astype(jnp.float32)
        y = (yf * jax.nn.silu(gate.astype(jnp.float32))).astype(x.dtype)
        x = x + y @ w_out[layer]
    return rmsnorm(x, final_norm_w)


_drawn_inputs = setup_inputs


def setup_inputs(seed=0):
    import zlib

    import numpy as np

    out = dict(_drawn_inputs(seed))
    spreads = {}
    factors = {'norm_w': 3.402,
     'b_forget': 3.965,
     'mem_norm_w': 7.793,
     'out_norm_w': 5.732,
     'final_norm_w': 2.849}
    for name, (base, spread) in spreads.items():
        noise = np.random.default_rng([zlib.crc32(name.encode()), seed]).standard_normal(out[name].shape)
        drawn = base * np.exp(spread * noise) if base else spread * noise
        out[name] = __import__('jax').numpy.asarray(drawn.astype(out[name].dtype))
    for name, factor in factors.items():
        out[name] = (out[name] * factor).astype(out[name].dtype)
    return out
```

```python
from contextlib import ExitStack

import concourse.bass as bass
from concourse import mybir

ALU = mybir.AluOpType
ACT = mybir.ActivationFunctionType
AX_X = mybir.AxisListType.X
F32 = mybir.dt.float32
F32R = mybir.dt.float32r
I32 = mybir.dt.int32

P = 128
D = 1024
S = 1024
KT = D // P
NB = S // P
HD = 64
NPAIR = 4
MPAIR = 2
MEM = 256
MB = MEM // P
NT_OUT = 2 * NPAIR + MPAIR
FH = 8
CW = 512
EPS = 1e-6
SCALE = HD ** -0.5
LOWEST = -3.0e38

UNITS = 2 * NB
T_LAG, PV_LAG = 2, 3
STEPS = UNITS + PV_LAG

FIRST_TILES = 3
TURN_TILES = 8
MEM_TILE0 = FIRST_TILES + TURN_TILES * (NPAIR - 1) + 5
N_TILES = MEM_TILE0 + 2 * MPAIR + 2 * MPAIR
FIRST_PIECES = 2 * FIRST_TILES
TURN_PIECES = 20
RSQRT_STEPS = 4 + 3 * 4
TURN_STEPS = 2 * RSQRT_STEPS + 4 * 2 + 4 * 4 + 2 * 6

TILE_OF = {"Q": 0, "K": 1, "V": 2}


def tile_pieces(what, tile):
    return [(what, tile, 0, 8), (what, tile, 1, 8)]


SB_PIECES = [p for j, w in enumerate(["Q", "K", "V", "G0", "G1"]) for p in tile_pieces(w, j)]
FX_PIECES = [p for j, w in enumerate(["Q", "K", "V"]) for p in tile_pieces(w, j)]
LAST_PIECES = ([("memT", None, g, 1) for g in range(4)]
               + [("memK", 0, 0, 4), ("memK", 1, 1, 4), ("memV", 2, 0, 4), ("memV", 3, 1, 4)]
               + tile_pieces("memQ0", 4) + tile_pieces("memQ1", 5))
MEM_PIECES = [tile_pieces("memG0", 0), tile_pieces("memG1", 0)]


def plan(pieces, tail):
    inside = pieces[:len(pieces) - tail]
    total = sum(p[3] for p in inside)
    ends, at = [], 0
    for p in inside:
        at += p[3]
        ends.append(at)
    issued = [((s + 1) * total) // STEPS for s in range(STEPS)]
    parts = [issued[s] - (issued[s - 1] if s else 0) for s in range(STEPS)]
    done = [[q for q, e in enumerate(ends) if (issued[s - 1] if s else 0) < e <= issued[s]] for s in range(STEPS)]
    return parts, done, list(range(len(inside), len(pieces)))


class Causal:
    CHUNKS, GROUPS = 24, 24

    @staticmethod
    def width(tb):
        return (tb + 1) * P

    @staticmethod
    def before(u):
        h, tb = divmod(u, NB)
        return 12 * h + (tb if tb < 4 else 4 + 2 * (tb - 4))


class Memory:
    CHUNKS, GROUPS = UNITS, UNITS

    @staticmethod
    def width(tb):
        return MEM

    @staticmethod
    def before(u):
        return u


def spans(width):
    return [(c, min(c + CW, width)) for c in range(0, width, CW)]


def hybrid_layer(nc, x, mem, w_tiles, w_forget, w_out, norm_w, mem_norm_w, out_norm_w, b_forget,
                 final_norm_w, out):
    yT_dram = nc.dram_tensor("yT_dram", (NT_OUT, P, S), F32, kind="Internal").ap()
    negL_dram = nc.dram_tensor("negL_dram", (FH, S), F32, kind="Internal").ap()

    with ExitStack() as ctx:
        def sb(name, shape, dt=F32):
            return ctx.enter_context(nc.sbuf_tensor(name, shape, dt))

        def sem(name):
            return ctx.enter_context(nc.semaphore(name))

        hT = sb("hT", [P, 2, KT, S], F32R)
        sb_heads = sb("sb_heads", [P, 8 * S], F32R)
        fx_heads = sb("fx_heads", [P, 8 * S], F32R)
        w_raw = sb("w_raw", [P, KT * P])
        w_parts = sb("w_parts", [P, 2, 2, KT * P], F32R)
        pT = sb("pT", [P, 3, 2, CW], F32R)
        work = sb("work", [P, 6, S])
        negL = sb("negL", [P, 2, S])
        y = sb("y", [P, NB, 2, HD])
        silu = sb("silu", [P, 2, S])
        diag = sb("diag", [P, 2, P])
        o_tmp = sb("o_tmp", [P, 4, HD])
        ident = sb("ident", [P, P])
        out_g = sb("out_g", [P, NT_OUT])
        in_g = sb("in_g", [P, KT])
        mem_g = sb("mem_g", [P, KT])
        b_f = sb("b_f", [FH, 1])
        peak = sb("peak", [P, 8])
        npeak = sb("npeak", [P, UNITS])
        rowsum = sb("rowsum", [P, UNITS])
        rinv = sb("rinv", [P, 4])
        ssq = sb("ssq", [P, NB, 2])
        rs = sb("rs", [P, 3, UNITS])

        banks = ctx.enter_context(nc.psum_tensor("banks", [P, 8, CW], F32))
        S_BANK, T_BANK, O_BANK, PJ_BANK = 0, 3, 5, 6

        def q_of(region):
            return region[:, 0:2 * S].rearrange("p (h t) -> p h t", h=2)

        def k_of(region):
            return region[:, 2 * S:6 * S].rearrange("p (h l t) -> p h l t", h=2, l=2)

        def v_of(region):
            return region[:, 6 * S:8 * S].rearrange("p (b h c) -> p b h c", b=NB, h=2)

        mem_k = sb_heads[:, 0:2 * S].rearrange("p (h l t) -> p h l t", h=4, l=2)
        mem_q = sb_heads[:, 2 * S:6 * S].rearrange("p (h t) -> p h t", h=4)
        memT = sb_heads[:, 2 * S:6 * S].rearrange("p (l k t) -> p l k t", l=2, k=KT)
        mem_v = sb_heads[:, 6 * S:7 * S].rearrange("p (b h c) -> p b h c", b=MB, h=4)
        mem_row = silu[:, 0, :]
        forget_hi = fx_heads[:, 0:KT * FH]
        forget_lo = fx_heads[:, KT * FH:2 * KT * FH]
        wo_hl = ([fx_heads[:, 2 * S * j:2 * S * (j + 1)].rearrange("p (l n) -> p l n", l=2) for j in range(4)]
                 + [hT[:, 0, 2 * j:2 * j + 2, :] for j in range(4)] + [hT[:, 1, 2 * j:2 * j + 2, :] for j in range(2)])
        YW = NT_OUT * P
        y_hl = [sb_heads[:, 2 * YW * b:2 * YW * (b + 1)].rearrange("p (l j t) -> p l j t", l=2, j=NT_OUT) for b in range(2)]
        work_flat = work[:, :, :].rearrange("p a b -> p (a b)")
        y_raw = [work_flat[:, YW * b:YW * (b + 1)] for b in range(2)]
        res = [work_flat[:, 3 * S + S * b:3 * S + S * (b + 1)] for b in range(2)]
        final_g = y[:, :, :, :].rearrange("p a b c -> p (a b c)")

        consts_in, x_in, x_in2, w_in_dma, wf_in = sem("consts_in"), sem("x_in"), sem("x_in2"), sem("w_in_dma"), sem("wf_in")
        ident_zero, ident_done = sem("ident_zero"), sem("ident_done")
        x_ssq, x_rstd, x_scaled = sem("x_ssq"), sem("x_rstd"), sem("x_scaled")
        xT_ready, xT_hi, xT_lo = sem("xT_ready"), sem("xT_hi"), sem("xT_lo")
        wf_hi, wf_lo, f_logit = sem("wf_hi"), sem("wf_lo"), sem("f_logit")
        f_abs, f_exp, f_ln, f_scan, negL_out, negL_in = (sem("f_abs"), sem("f_exp"), sem("f_ln"), sem("f_scan"),
                                                         sem("negL_out"), sem("negL_in"))
        w_hi, w_lo = sem("w_hi"), sem("w_lo")
        piece_ready, piece_hi, piece_done, k_dup = sem("piece_ready"), sem("piece_hi"), sem("piece_done"), sem("k_dup")
        s_ready, sb_read, fx_read = sem("s_ready"), sem("sb_read"), sem("fx_read")
        fail_masked, beta_masked, scanned, sb_p = sem("fail_masked"), sem("beta_masked"), sem("scanned"), sem("sb_p")
        diag_ready, fx_max, fx_p = sem("diag_ready"), sem("fx_max"), sem("fx_p")
        t_ready, t_hi, t_lo, pv_done = sem("t_ready"), sem("t_hi"), sem("t_lo"), sem("pv_done")
        o_lo, o_read, y_ready, y_out = sem("o_lo"), sem("o_read"), sem("y_ready"), sem("y_out")
        gate_sig = sem("gate_sig")
        mem_in, mem_ssq, mem_rstd, mem_scaled, mem_evac = (sem("mem_in"), sem("mem_ssq"), sem("mem_rstd"),
                                                           sem("mem_scaled"), sem("mem_evac"))
        wo_in, wo_hi, wo_lo = sem("wo_in"), sem("wo_hi"), sem("wo_lo")
        yb_in, xb_in, fin_in = [sem("yb_in0"), sem("yb_in1")], [sem("xb_in0"), sem("xb_in1")], sem("fin_in")
        yb_hi, yb_lo, proj_out, res_sum, res_ssq, res_done = (sem("yb_hi"), sem("yb_lo"), sem("proj_out"), sem("res_sum"),
                                                              sem("res_ssq"), sem("res_done"))
        stored = [sem("stored0"), sem("stored1")]
        dve_step = sem("dve_step")

        def tile_no(kind, it, j):
            if kind == "sb":
                return it * TURN_TILES + (FIRST_TILES + j)
            if kind == "fx":
                return it * TURN_TILES + (FIRST_TILES + 5 + j)
            return MEM_TILE0 + j if kind == "last" else MEM_TILE0 + 6 + it
        SB_N, FX_N, LAST_N, MM_N = 12, 8, 14, 4

        def piece_no(kind, it, q):
            if kind == "sb":
                return it * TURN_PIECES + (FIRST_PIECES + q)
            if kind in ("fx", "last"):
                return it * TURN_PIECES + (FIRST_PIECES + SB_N + q)
            return FIRST_PIECES + (NPAIR - 1) * TURN_PIECES + SB_N + LAST_N + MM_N * it + q

        def hi_no(kind, it, q):
            turn = TURN_PIECES - 4
            if kind == "sb":
                return it * turn + (FIRST_PIECES + q)
            if kind in ("fx", "last"):
                return it * turn + (FIRST_PIECES + SB_N - 2 + q)
            return FIRST_PIECES + (NPAIR - 1) * turn + SB_N - 2 + LAST_N - 2 + (MM_N - 2) * it + q

        def bank_of(kind, it, q):
            return PJ_BANK + q % 2

        def chunk_no(kind, it, g):
            return it * 48 + g if kind == "sb" else it * 48 + (24 + g) if kind != "mm" else 192 + 16 * it + g

        group_no = chunk_no

        def ring(kind, it, g, n):
            return g % n if kind != "mm" else (192 + 16 * it + g) % n

        def unit_no(kind, it, u):
            return it * UNITS + u if kind != "mm" else (NPAIR + it) * UNITS + u

        def half_no(kind, it, h):
            return it * 8 + h if kind == "sb" else it * 8 + (4 + h) if kind != "mm" else 32 + 4 * it + h

        def pair_no(kind, it):
            return it * 2 if kind == "sb" else it * 2 + 1 if kind != "mm" else 8 + it

        def out_tile(kind, it):
            return it if kind == "sb" else it + NPAIR if kind != "mm" else 2 * NPAIR + it

        def geometry(kind):
            return Memory if kind == "mm" else Causal

        def pieces_of(kind, it):
            if kind == "sb":
                return SB_PIECES, 2
            if kind == "fx":
                return FX_PIECES, 2
            if kind == "last":
                return LAST_PIECES, 1
            return MEM_PIECES[it], 1

        def tile_parity(kind, it, j):
            if kind == "sb":
                return (FIRST_TILES + j) % 2
            if kind == "fx":
                return (FIRST_TILES + 5 + j) % 2
            return tile_no(kind, it, j) % 2

        def region_of(kind):
            return sb_heads if kind == "sb" else fx_heads

        def target_of(kind):
            return fx_heads if kind == "sb" else sb_heads

        def closes_tile(piece):
            return piece[1] is not None and (piece[0] in ("memK", "memV") or piece[2] == 1)

        def wait_alone(eng, what, value):
            value = value if isinstance(value, int) else eng.to_reg(value)
            eng.wait_ge(consts_in, 64)
            eng.wait_ge(what, value)

        block = ctx.enter_context(nc.Block())

        @block.sync
        def _(sp):
            def wait(what, value):
                wait_alone(sp, what, value)

            def load_tile(n):
                wait(w_hi, n)
                wait(w_lo, n)
                sp.dma_start(w_raw[:, :], w_tiles[bass.ds(n, 1), :, :]).then_inc(w_in_dma, 16)

            def copy_keys(region, n_piece):
                wait(piece_done, n_piece + 1)
                k = k_of(region)
                sp.dma_start(k[HD:P, 0, :, :].bitcast(F32), k[0:HD, 0, :, :].bitcast(F32)).then_inc(k_dup, 16)
                sp.dma_start(k[0:HD, 1, :, :].bitcast(F32), k[HD:P, 1, :, :].bitcast(F32)).then_inc(k_dup, 16)

            def phase(kind, it):
                pieces, _ = pieces_of(kind, it)
                if kind == "sb":
                    for h in range(2):
                        sp.dma_start(negL[:, h, :], negL_dram[bass.ds(it * 2 + h, 1), :].broadcast_to((P, S))
                                     ).then_inc(negL_in, 16)
                tiles = 0
                for q, piece in enumerate(pieces):
                    if piece[0] == "memT" and piece[2] == 0:
                        for b in range(MB):
                            sp.dma_start(work[:, 2 + b, :], mem[0, b * P:(b + 1) * P, :]).then_inc(mem_in, 16)
                    if closes_tile(piece):
                        n = tile_no(kind, it, piece[1])
                        if kind in ("sb", "fx") or n + 3 < N_TILES:
                            load_tile(n + 3)
                        if piece[0] == "K":
                            copy_keys(target_of(kind), piece_no(kind, it, q))
                        tiles += 1
                        if tiles == 1 and kind in ("fx", "last"):
                            wait(y_out, (it * 2 + 1) * 16)
                if kind == "last":
                    for m, h in ((0, 0), (0, 1), (1, 2), (1, 3)):
                        mine, other = (slice(0, HD), slice(HD, P)) if h % 2 == 0 else (slice(HD, P), slice(0, HD))
                        wait(piece_done, piece_no(kind, it, 4 + m) + 1)
                        sp.dma_start(mem_k[other, h, :, :].bitcast(F32), mem_k[mine, h, :, :].bitcast(F32)).then_inc(k_dup, 16)
                wait(piece_done, piece_no(kind, it, len(pieces) + 1) + 1)
                side = 0 if kind == "sb" else 1 if kind != "mm" else it
                sp.dma_start(yT_dram[bass.ds(out_tile(kind, it), 1), :, :], silu[:, side, :]).then_inc(y_out, 16)
                if kind in ("fx", "last"):
                    wait(y_out, (it * 2 + 2) * 16)

            for dst, src in ((in_g, norm_w), (mem_g, mem_norm_w), (out_g, out_norm_w), (b_f, b_forget)):
                sp.dma_start(dst[:, :], src).then_inc(consts_in, 16)
            for b in range(4):
                sp.dma_start(work[:, b, :], x[0, b * P:(b + 1) * P, :]).then_inc(x_in, 16)
            sp.dma_start(w_raw[:, :], w_tiles[0, :, :]).then_inc(w_in_dma, 16)
            sp.dma_start(diag[:, 0, 0:KT * FH], w_forget).then_inc(wf_in, 16)
            load_tile(1)
            sp.wait_ge(xT_ready, KT)
            for b in range(4):
                sp.dma_start(work[:, b, :], x[0, (4 + b) * P:(5 + b) * P, :]).then_inc(x_in2, 16)
            load_tile(2)
            load_tile(3)
            load_tile(4)
            copy_keys(sb_heads, 3)
            load_tile(5)
            sp.wait_ge(f_scan, 1)
            sp.dma_start(negL_dram[:, :], work[0:FH, 5, :]).then_inc(negL_out, 16)
            sp.wait_ge(negL_out, 16)
            with sp.Fori(0, NPAIR - 1) as it:
                phase("sb", it)
                phase("fx", it)
            phase("sb", NPAIR - 1)
            phase("last", NPAIR - 1)
            for j in range(NT_OUT):
                if j == 0:
                    sp.wait_ge(w_hi, N_TILES)
                    sp.wait_ge(w_lo, N_TILES)
                    phase("mm", 0)
                    phase("mm", 1)
                else:
                    sp.wait_ge(wo_hi, j)
                    sp.wait_ge(wo_lo, j)
                sp.dma_start(w_raw[:, :], w_out[j * P:(j + 1) * P, :]).then_inc(wo_in, 16)
                if j == 0:
                    sp.wait_ge(y_out, 16 * NT_OUT)
                    for b in range(2):
                        sp.dma_start(y_raw[b].rearrange("p (j t) -> p j t", j=NT_OUT),
                                     yT_dram[:, :, b * P:(b + 1) * P].rearrange("j p t -> p j t")).then_inc(yb_in[b], 16)
                        sp.dma_start(res[b], x[0, b * P:(b + 1) * P, :]).then_inc(xb_in[b], 16)
                    sp.dma_start(final_g, final_norm_w.broadcast_to((P, D))).then_inc(fin_in, 16)
            for m in range(NB):
                b = m % 2
                if m + 2 < NB:
                    sp.wait_ge(yb_lo, m + 1)
                    sp.dma_start(y_raw[b].rearrange("p (j t) -> p j t", j=NT_OUT),
                                 yT_dram[:, :, (m + 2) * P:(m + 3) * P].rearrange("j p t -> p j t")
                                 ).then_inc(yb_in[b], 16)
                sp.wait_ge(res_done, m + 1)
                sp.dma_start(out[0, m * P:(m + 1) * P, :], res[b]).then_inc(stored[b], 16)
                if m + 2 < NB:
                    sp.wait_ge(stored[b], 16 * (m // 2 + 1))
                    sp.dma_start(res[b], x[0, (m + 2) * P:(m + 3) * P, :]).then_inc(xb_in[b], 16)
            for b in range(2):
                sp.wait_ge(stored[b], 16 * (NB // 2))

        @block.tensor
        def _(pe):
            def project(what, n, parity, c, bank):
                w = w_parts[:, parity, :, :].rearrange("p l (k c) -> p l k c", k=KT)
                pe.wait_ge(w_lo, n + 1)
                if what == "V":
                    for part in range(8):
                        b, k0 = part // 2, 4 * (part % 2)
                        tok = slice((4 * c + b) * P, (4 * c + b + 1) * P)
                        for k in range(k0, k0 + 4):
                            o = banks[:, bank, b * P:(b + 1) * P]
                            pe.matmul(o, hT[:, 0, k, tok], w[:, 0, k, :], start=(k == 0), stop=False)
                            pe.matmul(o, hT[:, 0, k, tok], w[:, 1, k, :], start=False, stop=False)
                            mm = pe.matmul(o, hT[:, 1, k, tok], w[:, 0, k, :], start=False, stop=(k == KT - 1))
                        if part == 7:
                            mm.then_inc(piece_ready, 1)
                        yield
                else:
                    tok = slice(c * CW, (c + 1) * CW)
                    for k in range(KT):
                        o = banks[:, bank, :]
                        pe.matmul(o, w[:, 0, k, :], hT[:, 0, k, tok], start=(k == 0), stop=False)
                        pe.matmul(o, w[:, 0, k, :], hT[:, 1, k, tok], start=False, stop=False)
                        mm = pe.matmul(o, w[:, 1, k, :], hT[:, 0, k, tok], start=False, stop=(k == KT - 1))
                        if k == KT - 1:
                            mm.then_inc(piece_ready, 1)
                        yield

            def parts_of(kind, it):
                pieces, _ = pieces_of(kind, it)
                for q, (what, tile, c, parts) in enumerate(pieces):
                    bank = bank_of(kind, it, q)
                    pe.wait_ge(piece_done, piece_no(kind, it, q) - 1)
                    if tile is not None:
                        parity = tile_parity(kind, it, tile)
                        n = tile_no(kind, it, tile)
                        w = w_parts[:, parity, :, :].rearrange("p l (k c) -> p l k c", k=KT)
                    if what == "memT":
                        pe.wait_ge(mem_scaled, MB)
                        for i in range(4):
                            k, b = 2 * c + i // 2, i % 2
                            mm = pe.transpose(banks[:, bank, i * P:(i + 1) * P], work[:, 2 + b, k * P:(k + 1) * P], ident[:, :])
                        mm.then_inc(piece_ready, 1)
                        yield
                    elif what == "memK":
                        pe.wait_ge(w_lo, n + 1)
                        pe.wait_ge(piece_done, piece_no(kind, it, 4))
                        for k in range(KT):
                            o = banks[:, bank, 0:MEM]
                            pe.matmul(o, w[:, 0, k, :], memT[:, 0, k, :], start=(k == 0), stop=False)
                            pe.matmul(o, w[:, 0, k, :], memT[:, 1, k, :], start=False, stop=False)
                            mm = pe.matmul(o, w[:, 1, k, :], memT[:, 0, k, :], start=False, stop=(k == KT - 1))
                            if k == KT - 1:
                                mm.then_inc(piece_ready, 1)
                            if k % 2:
                                yield
                    elif what == "memV":
                        pe.wait_ge(w_lo, n + 1)
                        for b in range(MB):
                            tok = slice(b * P, (b + 1) * P)
                            for k in range(KT):
                                o = banks[:, bank, b * P:(b + 1) * P]
                                pe.matmul(o, memT[:, 0, k, tok], w[:, 0, k, :], start=(k == 0), stop=False)
                                pe.matmul(o, memT[:, 0, k, tok], w[:, 1, k, :], start=False, stop=False)
                                mm = pe.matmul(o, memT[:, 1, k, tok], w[:, 0, k, :], start=False, stop=(k == KT - 1))
                                if b == MB - 1 and k == KT - 1:
                                    mm.then_inc(piece_ready, 1)
                                if k % 4 == 3:
                                    yield
                    else:
                        yield from project(what, n, parity, c, bank)

            def scores(kind, it, u):
                h, tb = divmod(u, NB)
                geo = geometry(kind)
                q0 = slice(tb * P, (tb + 1) * P)
                if kind == "mm":
                    q = mem_q[:, 2 * it + h, q0]
                    k = mem_k[:, 2 * it + h, :, :]
                else:
                    q = q_of(region_of(kind))[:, h, q0]
                    k = k_of(region_of(kind))[:, h, :, :]
                for i, (c0, c1) in enumerate(spans(geo.width(tb))):
                    g = geo.before(u) + i
                    if g >= 3:
                        if kind == "sb":
                            pe.wait_ge(sb_read, it * 24 + (g - 2))
                        elif kind == "mm":
                            pe.wait_ge(fx_p, unit_no(kind, it, g) - 2)
                        else:
                            pe.wait_ge(fx_read, it * 24 + (g - 2))
                    o = banks[:, S_BANK + ring(kind, it, g, 3), 0:c1 - c0]
                    pe.matmul(o, q, k[:, 0, c0:c1], start=True, stop=False)
                    pe.matmul(o, q, k[:, 1, c0:c1], start=False, stop=True).then_inc(s_ready, 1)

            def transposes(kind, it, u):
                h, tb = divmod(u, NB)
                geo = geometry(kind)
                n_sb = geo.width(tb) // P
                if kind == "sb":
                    pe.wait_ge(sb_p, unit_no(kind, it, u) + 1)
                    p = work[:, 2 + u % 2, :]
                else:
                    pe.wait_ge(fx_p, unit_no(kind, it, u) + 1)
                    p = work[:, u % 2, :]
                for i in range((n_sb + 3) // 4):
                    g = geo.before(u) + i
                    if g >= 2:
                        pe.wait_ge(t_lo, group_no(kind, it, g) - 1)
                    for s in range(4 * i, min(4 * i + 4, n_sb)):
                        mm = pe.transpose(banks[:, T_BANK + ring(kind, it, g, 2), (s - 4 * i) * P:(s - 4 * i + 1) * P],
                                          p[:, s * P:(s + 1) * P], ident[:, :])
                    mm.then_inc(t_ready, 1)

            def values(kind, it, u):
                h, tb = divmod(u, NB)
                geo = geometry(kind)
                n_sb = geo.width(tb) // P
                v = mem_v[:, :, 2 * it + h, :] if kind == "mm" else v_of(region_of(kind))[:, :, h, :]
                half = u // 4
                if u % 4 == 0 and half:
                    pe.wait_ge(o_read, half_no(kind, it, half))
                o = (tb % 4) * P
                for i in range((n_sb + 3) // 4):
                    g = geo.before(u) + i
                    pe.wait_ge(t_lo, group_no(kind, it, g) + 1)
                    for s in range(4 * i, min(4 * i + 4, n_sb)):
                        part = pT[:, ring(kind, it, g, 3), :, (s - 4 * i) * P:(s - 4 * i + 1) * P]
                        pe.matmul(banks[:, O_BANK, o:o + P], part[:, 0, :], v[:, s, :], start=(s == 0), stop=(s == n_sb - 1))
                        mm = pe.matmul(banks[:, O_BANK, o:o + HD], part[:, 1, :], v[:, s, 0:HD], start=False,
                                       stop=(s == n_sb - 1), skip_group_check=True)
                    mm.then_inc(pv_done, 1)

            def phase(kind, it):
                pieces, tail = pieces_of(kind, it)
                issue, done, last = plan(pieces, tail)
                if kind == "sb":
                    pe.wait_ge(piece_done, it * TURN_PIECES + FIRST_PIECES)
                    pe.wait_ge(k_dup, it * 64 + 32)
                elif kind == "mm":
                    pe.wait_ge(k_dup, 256 + 64)
                else:
                    pe.wait_ge(k_dup, it * 64 + 64)
                    pe.wait_ge(piece_done, it * TURN_PIECES + (FIRST_PIECES + 6))
                if kind == "mm" and it == 0:
                    pe.wait_ge(piece_done, piece_no("last", NPAIR - 1, LAST_N - 1) + 1)
                work_left = parts_of(kind, it)
                for i in range(STEPS):
                    if i < UNITS:
                        scores(kind, it, i)
                    for _ in range(issue[i]):
                        next(work_left)
                    if T_LAG <= i < UNITS + T_LAG:
                        transposes(kind, it, i - T_LAG)
                    if PV_LAG <= i:
                        values(kind, it, i - PV_LAG)
                for _ in work_left:
                    pass
                pe.wait_ge(y_ready, pair_no(kind, it) + 1)
                for c in range(2):
                    q = len(pieces) + c
                    pe.wait_ge(piece_done, piece_no(kind, it, q) - 1)
                    for b in range(4):
                        mm = pe.transpose(banks[:, bank_of(kind, it, q), b * P:(b + 1) * P],
                                          y[:, 4 * c + b, :, :].rearrange("p h c -> p (h c)"), ident[:, :])
                    mm.then_inc(piece_ready, 1)

            pe.wait_ge(ident_done, 1)
            for c in range(2):
                pe.wait_ge(x_scaled, 4 * (c + 1))
                for k in range(KT):
                    g = c * KT + k
                    if g >= 2:
                        pe.wait_ge(xT_lo, g - 1)
                    for b in range(4):
                        mm = pe.transpose(banks[:, T_BANK + g % 2, b * P:(b + 1) * P], work[:, b, k * P:(k + 1) * P], ident[:, :])
                    mm.then_inc(xT_ready, 1)
            pe.wait_ge(xT_lo, 2 * KT)
            pe.wait_ge(wf_lo, 1)
            for c in range(2):
                tok = slice(c * CW, (c + 1) * CW)
                for k in range(KT):
                    f = slice(k * FH, (k + 1) * FH)
                    o = banks[0:FH, S_BANK + c, :]
                    pe.matmul(o, forget_hi[:, f], hT[:, 0, k, tok], start=(k == 0), stop=False)
                    pe.matmul(o, forget_hi[:, f], hT[:, 1, k, tok], start=False, stop=False)
                    mm = pe.matmul(o, forget_lo[:, f], hT[:, 0, k, tok], start=False, stop=(k == KT - 1))
                mm.then_inc(f_logit, 1)
            for q in range(FIRST_PIECES):
                if q >= 2:
                    pe.wait_ge(piece_done, q - 1)
                for _ in project("QKV"[q // 2], q // 2, (q // 2) % 2, q % 2, PJ_BANK + q % 2):
                    pass
            pe.wait_ge(negL_out, 16)
            with pe.Fori(0, NPAIR - 1) as it:
                phase("sb", it)
                phase("fx", it)
            phase("sb", NPAIR - 1)
            phase("last", NPAIR - 1)
            phase("mm", 0)
            phase("mm", 1)
            for m in range(NB):
                b = m % 2
                pe.wait_ge(yb_lo, m + 1)
                if m >= 2:
                    pe.wait_ge(res_sum, m - 1)
                for j in range(NT_OUT):
                    if m == 0:
                        pe.wait_ge(wo_lo, j + 1)
                    for l, r in ((0, 0), (0, 1), (1, 0)):
                        for c in range(2):
                            mm = pe.matmul(banks[:, 2 * b + c, :], y_hl[b][:, l, j, :], wo_hl[j][:, r, c * CW:(c + 1) * CW],
                                           start=(j == 0 and (l, r) == (0, 0)), stop=(j == NT_OUT - 1 and l == 1))
                mm.then_inc(proj_out, 1)

        @block.scalar
        def _(act):
            def split_hi(n, parity):
                act.wait_ge(w_in_dma, (n + 1) * 16)
                act.activation(w_parts[:, parity, 0, :], w_raw[:, :], ACT.Copy).then_inc(w_hi, 1)

            def evacuate(kind, it, piece, q_no, bank):
                what, tile, c, _ = piece
                act.wait_ge(piece_ready, q_no + 1)
                src = banks[:, bank, :]
                cols = slice(c * CW, (c + 1) * CW)
                if what == "Q":
                    q = q_of(target_of(kind))
                    act.activation(q[0:HD, 0, cols], src[0:HD], ACT.Copy, scale=SCALE)
                    ins = act.activation(q[HD:P, 1, cols], src[HD:P], ACT.Copy, scale=SCALE)
                elif what == "K":
                    k = k_of(target_of(kind))
                    act.activation(k[0:HD, 0, 0, cols], src[0:HD], ACT.Copy)
                    ins = act.activation(k[HD:P, 1, 0, cols], src[HD:P], ACT.Copy)
                elif what == "V":
                    ins = act.activation(v_of(target_of(kind))[:, 4 * c:4 * c + 4, :, 0:HD],
                                         src.rearrange("p (b h c) -> p b h c", b=4, h=2), ACT.Copy)
                elif what in ("G0", "G1", "memG0", "memG1"):
                    if what in ("memG0", "memG1"):
                        act.wait_ge(y_out, 16 * (2 * NPAIR - 1 + int(what[-1])))
                    ins = act.activation(silu[:, int(what[-1]), cols], src, ACT.Sigmoid)
                elif what == "memT":
                    for i in range(2):
                        k = 2 * c + i
                        ins = act.activation(memT[:, 0, k, :], src[:, i * MEM:(i + 1) * MEM], ACT.Copy, scale=mem_g[:, k:k + 1])
                elif what == "memK":
                    act.activation(mem_k[0:HD, 2 * c, 0, :], src[0:HD, 0:MEM], ACT.Copy)
                    ins = act.activation(mem_k[HD:P, 2 * c + 1, 0, :], src[HD:P, 0:MEM], ACT.Copy)
                elif what == "memV":
                    for b in range(MB):
                        ins = act.activation(mem_v[:, b, 2 * c:2 * c + 2, 0:HD],
                                             src[:, b * P:(b + 1) * P].rearrange("p (h c) -> p h c", h=2), ACT.Copy)
                elif what in ("memQ0", "memQ1"):
                    h = 2 * int(what[-1])
                    act.activation(mem_q[0:HD, h, cols], src[0:HD], ACT.Copy, scale=SCALE)
                    ins = act.activation(mem_q[HD:P, h + 1, cols], src[HD:P], ACT.Copy, scale=SCALE)
                ins.then_inc(piece_hi, 1)

            def evacuate_and_split(kind, it, q):
                pieces, _ = pieces_of(kind, it)
                evacuate(kind, it, pieces[q], piece_no(kind, it, q), bank_of(kind, it, q))
                if closes_tile(pieces[q]):
                    n = tile_no(kind, it, pieces[q][1])
                    if kind in ("sb", "fx") or n + 2 < N_TILES:
                        split_hi(n + 2, tile_parity(kind, it, pieces[q][1]))

            def sigmoids(it, u):
                h, tb = divmod(u, NB)
                if u >= 2:
                    act.wait_ge(scanned, it * UNITS + (u - 1))
                    act.wait_ge(t_ready, it * 48 + (Causal.before(u - 2) + (2 if (u - 2) % NB >= 4 else 1)))
                for i, (c0, c1) in enumerate(spans(Causal.width(tb))):
                    g = Causal.before(u) + i
                    act.wait_ge(s_ready, chunk_no("sb", it, g) + 1)
                    src = banks[:, S_BANK + g % 3, 0:c1 - c0]
                    act.activation(work[:, u % 2, c0:c1], src, ACT.Sigmoid, scale=-1.0)
                    act.activation(work[:, 2 + u % 2, c0:c1], src, ACT.Sigmoid).then_inc(sb_read, 1)

            def exponentials(kind, it, u):
                act.wait_ge(fx_max, unit_no(kind, it, u) + 1)
                h, tb = divmod(u, NB)
                p = work[:, u % 2, 0:geometry(kind).width(tb)]
                if kind == "mm":
                    if u >= 2:
                        act.wait_ge(t_ready, group_no(kind, it, u - 2) + 1)
                    act.activation(p, banks[:, S_BANK + ring(kind, it, u, 3), 0:MEM], ACT.Exp, bias=npeak[:, u:u + 1],
                                   accum_out=rowsum[:, u:u + 1]).then_inc(fx_p, 1)
                else:
                    act.activation(p, p, ACT.Exp, bias=npeak[:, u:u + 1], accum_out=rowsum[:, u:u + 1]).then_inc(fx_p, 1)

            def upper_parts(kind, it, u):
                geo = geometry(kind)
                n_sb = geo.width(u % NB) // P
                for i in range((n_sb + 3) // 4):
                    g = geo.before(u) + i
                    n = min(4, n_sb - 4 * i) * P
                    act.wait_ge(t_ready, group_no(kind, it, g) + 1)
                    if g >= 3:
                        act.wait_ge(pv_done, group_no(kind, it, g) - 2)
                    act.activation(pT[:, ring(kind, it, g, 3), 0, 0:n], banks[:, T_BANK + ring(kind, it, g, 2), 0:n],
                                   ACT.Copy).then_inc(t_hi, 1)

            def output_lo(kind, it, half):
                geo = geometry(kind)
                last = geo.before(4 * half + 3) + (1 if kind != "mm" and half % 2 else 0)
                act.wait_ge(pv_done, group_no(kind, it, last) + 1)
                if half:
                    act.wait_ge(o_read, half_no(kind, it, half))
                act.activation(o_tmp[:, :, :], banks[:, O_BANK, :].rearrange("p (b c) -> p b c", b=4)[:, :, HD:P],
                               ACT.Copy).then_inc(o_lo, 1)

            def phase(kind, it):
                pieces, tail = pieces_of(kind, it)
                issue, done, last = plan(pieces, tail)
                if kind == "last":
                    for b in range(MB):
                        act.wait_ge(mem_in, 16 * MB)
                        act.activation(work[:, 4, :], work[:, 2 + b, :], ACT.Square, accum_out=rs[:, 2, b:b + 1]).then_inc(mem_ssq, 1)
                        act.wait_ge(mem_ssq, b + 1)
                    act.wait_ge(mem_rstd, 1)
                    for b in range(MB):
                        act.activation(work[:, 2 + b, :], work[:, 2 + b, :], ACT.Copy, scale=rs[:, 1, b:b + 1]).then_inc(mem_scaled, 1)
                for i in range(STEPS):
                    if i < UNITS:
                        if kind == "sb":
                            sigmoids(it, i)
                        else:
                            exponentials(kind, it, i)
                    for q in done[i]:
                        evacuate_and_split(kind, it, q)
                    if T_LAG <= i < UNITS + T_LAG:
                        upper_parts(kind, it, i - T_LAG)
                    if PV_LAG <= i and (i - PV_LAG) % 4 == 3:
                        output_lo(kind, it, (i - PV_LAG) // 4)
                for q in last:
                    evacuate_and_split(kind, it, q)

            act.wait_ge(w_in_dma, 16)
            act.activation(w_parts[:, 0, 0, :], w_raw[:, :], ACT.Copy).then_inc(w_hi, 1)
            for b in range(NB):
                if b < 4:
                    act.wait_ge(x_in, 64)
                else:
                    act.wait_ge(x_in2, 64)
                act.activation(work[:, 4, :], work[:, b % 4, :], ACT.Square, accum_out=ssq[:, b, 0:1]).then_inc(x_ssq, 1)
                act.wait_ge(x_ssq, b + 1)
                if b % 4 == 3:
                    act.wait_ge(x_rstd, b // 4 + 1)
                    for i in range(4):
                        act.activation(work[:, i, :], work[:, i, :], ACT.Copy, scale=rs[:, 1, b - 3 + i:b - 2 + i]).then_inc(x_scaled, 1)
                    act.wait_ge(consts_in, 64)
                    for k in range(KT):
                        g = (b // 4) * KT + k
                        act.wait_ge(xT_ready, g + 1)
                        act.activation(hT[:, 0, k, (b // 4) * CW:(b // 4 + 1) * CW], banks[:, T_BANK + g % 2, :], ACT.Copy,
                                       scale=in_g[:, k:k + 1]).then_inc(xT_hi, 1)
                if b == 3:
                    split_hi(1, 1)
                    act.wait_ge(wf_in, 16)
                    act.activation(forget_hi, diag[:, 0, 0:KT * FH], ACT.Copy).then_inc(wf_hi, 1)
            act.wait_ge(f_abs, 1)
            act.activation(work[0:FH, 2, :], work[0:FH, 1, :], ACT.Exp, scale=-1.0).then_inc(f_exp, 1)
            act.wait_ge(f_exp, 1)
            act.activation(work[0:FH, 3, :], work[0:FH, 2, :], ACT.Ln, bias=1.0).then_inc(f_ln, 1)
            for q in range(FIRST_PIECES):
                evacuate("fx", 0, ("QKV"[q // 2], q // 2, q % 2, 8), q, PJ_BANK + q % 2)
                if q % 2:
                    split_hi(q // 2 + 2, (q // 2) % 2)
            with act.Fori(0, NPAIR - 1) as it:
                phase("sb", it)
                phase("fx", it)
            phase("sb", NPAIR - 1)
            phase("last", NPAIR - 1)
            phase("mm", 0)
            phase("mm", 1)
            for j in range(NT_OUT):
                act.wait_ge(wo_in, 16 * (j + 1))
                act.activation(wo_hl[j][:, 0, :], w_raw[:, :], ACT.Copy).then_inc(wo_hi, 1)
                if j == 0:
                    for m in range(2):
                        act.wait_ge(yb_in[m], 16)
                        act.activation(y_hl[m][:, 0, :, :], y_raw[m].rearrange("p (j t) -> p j t", j=NT_OUT), ACT.Copy).then_inc(yb_hi, 1)
            for m in range(NB):
                act.wait_ge(res_sum, m + 1)
                if m:
                    act.wait_ge(res_ssq, m)
                act.activation(silu[:, 0, :], res[m % 2], ACT.Square, accum_out=rs[:, 2, 0:1]).then_inc(res_ssq, 1)
                if m + 2 < NB:
                    act.wait_ge(yb_in[m % 2], 16 * (m // 2 + 2))
                    act.wait_ge(proj_out, m + 1)
                    act.activation(y_hl[m % 2][:, 0, :, :], y_raw[m % 2].rearrange("p (j t) -> p j t", j=NT_OUT), ACT.Copy).then_inc(yb_hi, 1)

        @block.gpsimd
        def _(pool):
            fill_one, fill_zero, fill_lowest = pool.to_reg(1.0), pool.to_reg(0.0), pool.to_reg(LOWEST)

            def split_lo(n, parity):
                pool.wait_ge(w_hi, n + 1)
                pool.tensor_tensor(w_parts[:, parity, 1, :], w_raw[:, :], w_parts[:, parity, 0, :].bitcast(F32),
                                   ALU.subtract).then_inc(w_lo, 1)

            def masks(it, u):
                h, tb = divmod(u, NB)
                wait_alone(pool, sb_read, it * 24 + (Causal.before(u) + (2 if tb >= 4 else 1)))
                blk = slice(tb * P, (tb + 1) * P)
                f, b = work[:, u % 2, blk], work[:, 2 + u % 2, blk]
                pool.affine_select(out=f, in_=f, compare_op=ALU.is_gt, fill=fill_one, base=0, pattern=[[-1, P]],
                                   channel_multiplier=1).then_inc(fail_masked, 1)
                pool.affine_select(out=b, in_=b, compare_op=ALU.is_gt, fill=fill_zero, base=0, pattern=[[-1, P]],
                                   channel_multiplier=1).then_inc(beta_masked, 1)

            def weights(it, u):
                h, tb = divmod(u, NB)
                w = Causal.width(tb) - 1
                b = work[:, 2 + u % 2, 0:w]
                pool.wait_ge(scanned, it * UNITS + (u + 1))
                pool.wait_ge(beta_masked, it * UNITS + (u + 1))
                pool.tensor_tensor(b, b, work[:, 4 + u % 2, 0:w], ALU.mult).then_inc(sb_p, 1)

            def diagonal(kind, it, u):
                h, tb = divmod(u, NB)
                if u >= 2:
                    wait_alone(pool, fx_read, it * 24 + (Causal.before(u - 2) + (2 if (u - 2) % NB >= 4 else 1)))
                pool.affine_select(out=diag[:, u % 2, :], in_=negL[:, h, tb * P:(tb + 1) * P], compare_op=ALU.is_ge,
                                   fill=fill_lowest, base=0, pattern=[[-1, P]], channel_multiplier=1).then_inc(diag_ready, 1)

            def maybe_split(kind, it, q):
                pieces, _ = pieces_of(kind, it)
                if closes_tile(pieces[q]):
                    n = tile_no(kind, it, pieces[q][1])
                    if kind in ("sb", "fx") or n + 2 < N_TILES:
                        split_lo(n + 2, tile_parity(kind, it, pieces[q][1]))

            def phase(kind, it):
                pieces, tail = pieces_of(kind, it)
                issue, done, last = plan(pieces, tail)
                if kind in ("fx", "last"):
                    wait_alone(pool, negL_in, (it + 1) * 32)
                for i in range(STEPS):
                    if kind == "sb":
                        if i < UNITS:
                            masks(it, i)
                        if 1 <= i <= UNITS:
                            weights(it, i - 1)
                    elif kind != "mm" and i < UNITS:
                        diagonal(kind, it, i)
                    for q in done[i]:
                        maybe_split(kind, it, q)
                for q in last:
                    maybe_split(kind, it, q)

            pool.memset(ident[:, :], 0.0).then_inc(ident_zero, 1)
            pool.wait_ge(ident_zero, 1)
            pool.affine_select(out=ident[:, :], in_=ident[:, :], compare_op=ALU.not_equal, fill=1.0, base=0,
                               pattern=[[-1, P]], channel_multiplier=1).then_inc(ident_done, 1)
            split_lo(0, 0)
            split_lo(1, 1)
            pool.wait_ge(wf_hi, 1)
            pool.tensor_tensor(forget_lo, diag[:, 0, 0:KT * FH], forget_hi.bitcast(F32), ALU.subtract).then_inc(wf_lo, 1)
            for t in range(FIRST_TILES):
                split_lo(t + 2, t % 2)
            with pool.Fori(0, NPAIR - 1) as it:
                phase("sb", it)
                phase("fx", it)
            phase("sb", NPAIR - 1)
            phase("last", NPAIR - 1)
            phase("mm", 0)
            phase("mm", 1)
            for j in range(NT_OUT):
                pool.wait_ge(wo_hi, j + 1)
                pool.tensor_tensor(wo_hl[j][:, 1, :], w_raw[:, :], wo_hl[j][:, 0, :].bitcast(F32), ALU.subtract).then_inc(wo_lo, 1)

        @block.vector
        def _(dve):
            steps = {"base": 0, "n": 0}

            def link(ins):
                steps["n"] += 1
                ins.then_inc(dve_step, 1)
                dve.wait_ge(dve_step, steps["base"] + steps["n"])

            def rsqrt(v, n, mean, last=None):
                r, half, t = rs[:, 0, 0:n], rs[:, 2, 0:n], rs[:, 1, 0:n]
                link(dve.tensor_scalar(half, v, 1.0 / mean, EPS, ALU.mult, ALU.add))
                link(dve.tensor_scalar(t.bitcast(I32), half.bitcast(I32), 1, None, ALU.logical_shift_right))
                link(dve.tensor_scalar(r.bitcast(I32), t.bitcast(I32), -1.0, float(0x5F3759DF), ALU.mult, ALU.add))
                link(dve.tensor_scalar(half, half, -0.5, None, ALU.mult))
                for _ in range(4):
                    link(dve.tensor_tensor(t, r, r, ALU.mult))
                    link(dve.tensor_tensor(t, t, half, ALU.mult))
                    link(dve.scalar_tensor_tensor(out=r, in0=t, scalar=1.5, in1=r, op0=ALU.add, op1=ALU.mult))

            def evacuate(kind, piece, n_hi, bank):
                what, tile, c, _ = piece
                dve.wait_ge(piece_hi, n_hi + 1)
                src = banks[:, bank, :]
                cols = slice(c * CW, (c + 1) * CW)

                def scaled(dst, s, hi):
                    return dve.scalar_tensor_tensor(out=dst, in0=s, scalar=SCALE, in1=hi.bitcast(F32), op0=ALU.mult, op1=ALU.subtract)

                if what == "Q":
                    q = q_of(target_of(kind))
                    scaled(q[HD:P, 0, cols], src[0:HD], q[0:HD, 0, cols])
                    ins = scaled(q[0:HD, 1, cols], src[HD:P], q[HD:P, 1, cols])
                elif what == "K":
                    k = k_of(target_of(kind))
                    dve.tensor_tensor(k[0:HD, 0, 1, cols], src[0:HD], k[0:HD, 0, 0, cols].bitcast(F32), ALU.subtract)
                    ins = dve.tensor_tensor(k[HD:P, 1, 1, cols], src[HD:P], k[HD:P, 1, 0, cols].bitcast(F32), ALU.subtract)
                elif what == "V":
                    v = v_of(target_of(kind))[:, 4 * c:4 * c + 4, :, :]
                    ins = dve.tensor_tensor(v[:, :, :, HD:P], src.rearrange("p (b h c) -> p b h c", b=4, h=2),
                                            v[:, :, :, 0:HD].bitcast(F32), ALU.subtract)
                elif what in ("G0", "G1", "memG0", "memG1"):
                    g = silu[:, int(what[-1]), cols]
                    ins = dve.tensor_tensor(g, src, g, ALU.mult)
                elif what == "memT":
                    for i in range(2):
                        k = 2 * c + i
                        ins = dve.scalar_tensor_tensor(out=memT[:, 1, k, :], in0=src[:, i * MEM:(i + 1) * MEM],
                                                       scalar=mem_g[:, k:k + 1], in1=memT[:, 0, k, :].bitcast(F32),
                                                       op0=ALU.mult, op1=ALU.subtract)
                elif what == "memK":
                    dve.tensor_tensor(mem_k[0:HD, 2 * c, 1, :], src[0:HD, 0:MEM], mem_k[0:HD, 2 * c, 0, :].bitcast(F32), ALU.subtract)
                    ins = dve.tensor_tensor(mem_k[HD:P, 2 * c + 1, 1, :], src[HD:P, 0:MEM],
                                            mem_k[HD:P, 2 * c + 1, 0, :].bitcast(F32), ALU.subtract)
                elif what == "memV":
                    for b in range(MB):
                        v = mem_v[:, b, 2 * c:2 * c + 2, :]
                        ins = dve.tensor_tensor(v[:, :, HD:P], src[:, b * P:(b + 1) * P].rearrange("p (h c) -> p h c", h=2),
                                                v[:, :, 0:HD].bitcast(F32), ALU.subtract)
                elif what in ("memQ0", "memQ1"):
                    h = 2 * int(what[-1])
                    scaled(mem_q[HD:P, h, cols], src[0:HD], mem_q[0:HD, h, cols])
                    ins = scaled(mem_q[0:HD, h + 1, cols], src[HD:P], mem_q[HD:P, h + 1, cols])
                ins.then_inc(piece_done, 1)

            def phase(kind, it):
                pieces, tail = pieces_of(kind, it)
                issue, done, last = plan(pieces, tail)
                geo = geometry(kind)

                def piece(q):
                    evacuate(kind, pieces[q], hi_no(kind, it, q), bank_of(kind, it, q))

                def scan(u):
                    w = Causal.width(u % NB)
                    dve.wait_ge(fail_masked, it * UNITS + (u + 1))
                    if u >= 2:
                        dve.wait_ge(sb_p, it * UNITS + (u - 1))
                    f = work[:, u % 2, w - 1:0:-1]
                    dve.tensor_tensor_scan(work[:, 4 + u % 2, w - 2::-1], f, f, 1.0, ALU.mult, ALU.bypass).then_inc(scanned, 1)

                def logits(u):
                    h, tb = divmod(u, NB)
                    if u >= 2:
                        dve.wait_ge(t_ready, group_no(kind, it, Causal.before(u - 2)) + (2 if (u - 2) % NB >= 4 else 1))
                    dve.wait_ge(diag_ready, it * UNITS + (u + 1))
                    start, n = LOWEST, 4 * (u % 2)
                    for i, (c0, c1) in enumerate(spans(Causal.width(tb))):
                        g = Causal.before(u) + i
                        wait_alone(dve, s_ready, chunk_no(kind, it, g) + 1)
                        cuts = [(a, b) for a, b in ((c0, min(c1, tb * P)), (max(c0, tb * P), c1)) if a < b]
                        for a, b in cuts:
                            bias = diag[:, u % 2, :] if a == tb * P else negL[:, h, a:b]
                            ins = dve.tensor_tensor_reduce(out=work[:, u % 2, a:b], in0=banks[:, S_BANK + g % 3, a - c0:b - c0],
                                                           in1=bias, scale=1.0, scalar=start, op0=ALU.add, op1=ALU.max,
                                                           accum_out=peak[:, n:n + 1])
                            start, n = peak[:, n:n + 1], n + 1
                            if b == c1:
                                ins.then_inc(fx_read, 1)
                                wait_alone(dve, fx_read, it * 24 + (g + 1))
                            else:
                                steps["n"] += 1
                                ins.then_inc(dve_step, 1)
                                wait_alone(dve, dve_step, steps["base"] + steps["n"])
                    dve.tensor_scalar(npeak[:, u:u + 1], start, -1.0, None, ALU.mult).then_inc(fx_max, 1)

                def mem_max(u):
                    dve.wait_ge(s_ready, chunk_no(kind, it, u) + 1)
                    top = peak[:, 4 * (u % 2):4 * (u % 2) + 1]
                    link(dve.reduce_max(top, banks[:, S_BANK + ring(kind, it, u, 3), 0:MEM], AX_X))
                    dve.tensor_scalar(npeak[:, u:u + 1], top, -1.0, None, ALU.mult).then_inc(fx_max, 1)

                def lower_parts(u):
                    n_sb = geo.width(u % NB) // P
                    for i in range((n_sb + 3) // 4):
                        g = geo.before(u) + i
                        n = min(4, n_sb - 4 * i) * P
                        dve.wait_ge(t_hi, group_no(kind, it, g) + 1)
                        part = pT[:, ring(kind, it, g, 3), :, 0:n]
                        dve.tensor_tensor(part[:, 1, :], banks[:, T_BANK + ring(kind, it, g, 2), 0:n], part[:, 0, :].bitcast(F32),
                                          ALU.subtract).then_inc(t_lo, 1)

                def output(half):
                    h, b0 = half // 2, 4 * (half % 2)
                    o = y[:, b0:b0 + 4, h, :]
                    dve.wait_ge(o_lo, half_no(kind, it, half) + 1)
                    link(dve.tensor_tensor(o, banks[:, O_BANK, :].rearrange("p (b c) -> p b c", b=4)[:, :, 0:HD], o_tmp[:, :, :], ALU.add))
                    if kind != "sb":
                        link(dve.reciprocal(rinv[:, :], rowsum[:, 4 * half:4 * half + 4]))
                        link(dve.tensor_tensor(o, o, rinv[:, :].unsqueeze(2).broadcast_to((P, 4, HD)), ALU.mult))
                    link(dve.tensor_tensor(o_tmp[:, :, :], o, o, ALU.mult))
                    dve.reduce_sum(ssq[:, b0:b0 + 4, h], o_tmp[:, :, :], AX_X).then_inc(o_read, 1)

                if kind == "last":
                    dve.wait_ge(mem_ssq, MB)
                    rsqrt(rs[:, 2, 0:MB], MB, D)
                    dve.tensor_copy(rs[:, 1, 0:MB], rs[:, 0, 0:MB]).then_inc(mem_rstd, 1)
                for i in range(STEPS):
                    if i < UNITS:
                        if kind == "sb":
                            scan(i)
                        elif kind == "mm":
                            mem_max(i)
                        else:
                            logits(i)
                    for q in done[i]:
                        piece(q)
                    if T_LAG <= i < UNITS + T_LAG:
                        lower_parts(i - T_LAG)
                    if PV_LAG <= i and (i - PV_LAG) % 4 == 3:
                        output((i - PV_LAG) // 4)
                dve.wait_ge(o_read, half_no(kind, it, 3) + 1)
                rsqrt(ssq[:, :, :].rearrange("p b h -> p (b h)"), UNITS, HD)
                yv = y[:, :, :, :].rearrange("p b h c -> p (b h) c")
                dve.tensor_tensor(yv, yv, rs[:, 0, :].unsqueeze(2).broadcast_to((P, UNITS, HD)), ALU.mult).then_inc(y_ready, 1)
                for q in last:
                    piece(q)
                side = 0 if kind == "sb" else 1 if kind != "mm" else it
                for c in range(2):
                    q = len(pieces) + c
                    dve.wait_ge(piece_ready, piece_no(kind, it, q) + 1)
                    g = silu[:, side, c * CW:(c + 1) * CW]
                    t = out_tile(kind, it)
                    dve.scalar_tensor_tensor(out=g, in0=banks[:, bank_of(kind, it, q), :], scalar=out_g[:, bass.ds(t, 1)], in1=g,
                                             op0=ALU.mult, op1=ALU.mult).then_inc(piece_done, 1)

            for c in range(2):
                dve.wait_ge(x_ssq, 4 * (c + 1))
                if c:
                    dve.wait_ge(x_scaled, 4)
                rsqrt(ssq[:, 4 * c:4 * c + 4, 0], 4, D)
                dve.tensor_copy(rs[:, 1, 4 * c:4 * c + 4], rs[:, 0, 0:4]).then_inc(x_rstd, 1)
                if c == 0:
                    dve.wait_ge(consts_in, 64)
                for k in range(KT):
                    g = c * KT + k
                    dve.wait_ge(xT_hi, g + 1)
                    cols = slice(c * CW, (c + 1) * CW)
                    dve.scalar_tensor_tensor(out=hT[:, 1, k, cols], in0=banks[:, T_BANK + g % 2, :], scalar=in_g[:, k:k + 1],
                                             in1=hT[:, 0, k, cols].bitcast(F32), op0=ALU.mult, op1=ALU.subtract).then_inc(xT_lo, 1)
            u, a, m, one, cum = (work[0:FH, i, :] for i in (0, 1, 4, 2, 5))
            dve.wait_ge(f_logit, 2)
            for c in range(2):
                link(dve.tensor_scalar(u[:, c * CW:(c + 1) * CW], banks[0:FH, S_BANK + c, :], b_f[:, 0:1], None, ALU.add))
            dve.scalar_tensor_tensor(out=a, in0=u, scalar=-1.0, in1=u, op0=ALU.mult, op1=ALU.max).then_inc(f_abs, 1)
            link(dve.tensor_scalar(m, u, -1.0, 0.0, ALU.mult, ALU.max))
            dve.wait_ge(f_ln, 1)
            link(dve.tensor_tensor(m, m, work[0:FH, 3, :], ALU.add))
            link(dve.memset(one, 1.0))
            dve.tensor_tensor_scan(cum, one, m, 0.0, ALU.mult, ALU.add).then_inc(f_scan, 1)
            for q in range(FIRST_PIECES):
                evacuate("fx", ("QKV"[q // 2], q // 2, q % 2, 8), q, PJ_BANK + q % 2)
            before_loop = steps["n"]
            with dve.Fori(0, NPAIR - 1) as it:
                steps["base"], steps["n"] = it * TURN_STEPS + before_loop, 0
                phase("sb", it)
                phase("fx", it)
                assert steps["n"] == TURN_STEPS, steps["n"]
            steps["base"], steps["n"] = before_loop + (NPAIR - 1) * TURN_STEPS, 0
            phase("sb", NPAIR - 1)
            phase("last", NPAIR - 1)
            phase("mm", 0)
            phase("mm", 1)
            for m in range(2):
                dve.wait_ge(yb_hi, m + 1)
                dve.tensor_tensor(y_hl[m][:, 1, :, :], y_raw[m].rearrange("p (j t) -> p j t", j=NT_OUT),
                                  y_hl[m][:, 0, :, :].bitcast(F32), ALU.subtract).then_inc(yb_lo, 1)
            dve.wait_ge(fin_in, 16)
            for m in range(NB):
                b = m % 2
                dve.wait_ge(proj_out, m + 1)
                dve.wait_ge(xb_in[b], 16 * (m // 2 + 1))
                for c in range(2):
                    r = res[b][:, c * CW:(c + 1) * CW]
                    ins = dve.tensor_tensor(r, banks[:, 2 * b + c, :], r, ALU.add)
                ins.then_inc(res_sum, 1)
                if m + 2 < NB:
                    dve.wait_ge(yb_hi, m + 3)
                    dve.tensor_tensor(y_hl[b][:, 1, :, :], y_raw[b].rearrange("p (j t) -> p j t", j=NT_OUT),
                                      y_hl[b][:, 0, :, :].bitcast(F32), ALU.subtract).then_inc(yb_lo, 1)
                dve.wait_ge(res_ssq, m + 1)
                rsqrt(rs[:, 2, 0:1], 1, D)
                dve.scalar_tensor_tensor(out=res[b], in0=res[b], scalar=rs[:, 0, 0:1], in1=final_g, op0=ALU.mult,
                                         op1=ALU.mult).then_inc(res_done, 1)


def kernel(x, mem, norm_w, w_in, b_forget, mem_norm_w, w_mem_kv, out_norm_w, w_out, final_norm_w):
    import numpy as np
    import concourse.bacc as bacc
    from concourse import mybir as mb
    from concourse.bass_utils import run_bass_kernel_spmd

    def tiles(w, starts):
        w = np.asarray(w)
        return [w[:, s:s + P].reshape(KT, P, P).transpose(1, 0, 2).reshape(P, KT * P) for s in starts]

    w = np.asarray(w_in)[0]
    sbw, gate0, mq0, f0 = 512, 3336, 3080, 3072
    qkv = lambda base, pair: [base + i * sbw + pair * P for i in range(3)]
    order = []
    for it in range(NPAIR):
        if it == 0:
            order += qkv(0, 0)
        order += qkv(3 * sbw, it) + [gate0 + it * P, gate0 + (NPAIR + it) * P]
        if it < NPAIR - 1:
            order += qkv(0, it + 1)
    w_tiles = tiles(w, order) + tiles(np.asarray(w_mem_kv)[0], [0, P, 2 * P, 3 * P])
    w_tiles += tiles(w, [mq0, mq0 + P, gate0 + 2 * NPAIR * P, gate0 + (2 * NPAIR + 1) * P])
    w_forget = w[:, f0:f0 + FH].reshape(KT, P, FH).transpose(1, 0, 2).reshape(P, KT * FH)
    arrays = {
        "in_x": np.asarray(x), "in_mem": np.asarray(mem), "in_w_tiles": np.stack(w_tiles), "in_w_forget": w_forget,
        "in_w_out": np.asarray(w_out)[0], "in_norm_w": np.asarray(norm_w).reshape(KT, P).T,
        "in_mem_norm_w": np.asarray(mem_norm_w).reshape(KT, P).T, "in_out_norm_w": np.asarray(out_norm_w).reshape(NT_OUT, P).T,
        "in_b_forget": np.asarray(b_forget).reshape(FH, 1), "in_final_norm_w": np.asarray(final_norm_w).reshape(1, D),
    }
    arrays = {k: np.ascontiguousarray(v) for k, v in arrays.items()}
    nc = bacc.Bacc("TRN2", target_bir_lowering=False, num_devices=1)
    args = [nc.dram_tensor(k, v.shape, mb.dt.from_np(v.dtype), kind="ExternalInput").ap() for k, v in arrays.items()]
    args.append(nc.dram_tensor("out_y", (1, S, D), F32, kind="ExternalOutput").ap())
    hybrid_layer(nc, *args)
    r = run_bass_kernel_spmd(nc, [arrays], core_ids=[0])
    return r.results[0]["out_y"]
```

```python
from contextlib import ExitStack

import concourse.bass as bass
from concourse import mybir

ALU = mybir.AluOpType
ACT = mybir.ActivationFunctionType
AX_X = mybir.AxisListType.X
F32 = mybir.dt.float32
F32R = mybir.dt.float32r
I32 = mybir.dt.int32

P = 128
D = 1024
S = 1024
KT = D // P
NB = S // P
HD = 64
NPAIR = 4
MPAIR = 2
MEM = 256
MB = MEM // P
NT_OUT = 2 * NPAIR + MPAIR
FH = 8
CW = 512
EPS = 1e-6
SCALE = HD ** -0.5
LOWEST = -3.0e38

UNITS = 2 * NB
EXP_LAG = 1
T_LAG, PV_LAG = 2, 3
RING = 3
LIGHT = 2.0
HEAD = 2

FIRST_TILES = 3
TURN_TILES = 8
MEM_TILE0 = FIRST_TILES + TURN_TILES * (NPAIR - 1) + 5
N_TILES = MEM_TILE0 + 2 * MPAIR + 2 * MPAIR
FIRST_PIECES = 2 * FIRST_TILES + 2
TURN_PIECES = 24
RSQRT_STEPS = 4 + 3 * 4
TURN_STEPS = 2 * RSQRT_STEPS + 4 * 1 + 4 * 3 + 2 * 6


def tile_pieces(what, tile):
    return [(what, tile, 0, 8), (what, tile, 1, 8)]


QKV_PIECES = tile_pieces("K", 0) + tile_pieces("Q", 1) + tile_pieces("V", 2) + [("VT", None, 0, 1), ("VT", None, 1, 1)]
SB_PIECES = QKV_PIECES + tile_pieces("G0", 3) + tile_pieces("G1", 4)
FX_PIECES = QKV_PIECES
LAST_PIECES = ([("memT", None, g, 1) for g in range(4)]
               + [("memK", 0, 0, 4), ("memK", 1, 1, 4), ("memV", 2, 0, 4), ("memV", 3, 1, 4)]
               + tile_pieces("memQ0", 4) + tile_pieces("memQ1", 5) + tile_pieces("memG0", 6))
PIECES = {"sb": SB_PIECES, "fx": FX_PIECES, "last": LAST_PIECES, "mm": tile_pieces("memG1", 7)}
TAIL = {"sb": 2, "fx": 3, "last": 2, "mm": 0}
N_UNITS = {"sb": UNITS, "fx": UNITS, "last": UNITS, "mm": 2 * UNITS}
STEPS = {k: n + PV_LAG for k, n in N_UNITS.items()}
MEM_STEP = 4
ACTIVE = {"sb": (HEAD, STEPS["sb"]), "fx": (HEAD, STEPS["fx"]), "last": (MEM_STEP + 2, STEPS["last"]), "mm": (HEAD, UNITS)}
WO_STEP = {2: 0, 5: 1, 8: 2, 11: 3, 17: 4, 20: 5, 23: 6, 26: 7, 29: 8, 32: 9}
Y_STEP = {18: 0, 24: 1}


def plan(kind):
    pieces, tail = PIECES[kind], TAIL[kind]
    n_steps = STEPS[kind]
    inside = pieces[:len(pieces) - tail]
    total = sum(p[3] for p in inside)
    ends, at = [], 0
    for p in inside:
        at += p[3]
        ends.append(at)
    first, behind = ACTIVE[kind]
    def weight(s):
        if not first <= s < behind:
            return 0
        return 1 if kind == "mm" else LIGHT - Causal.width(s) / S if s < UNITS else LIGHT
    weights = [weight(s) for s in range(n_steps)]
    issued = [round(total * sum(weights[:s + 1]) / sum(weights)) for s in range(n_steps)]
    parts = [issued[s] - (issued[s - 1] if s else 0) for s in range(n_steps)]
    done = [[q for q, e in enumerate(ends) if (issued[s - 1] if s else 0) < e <= issued[s]] for s in range(n_steps)]
    return parts, done, list(range(len(inside), len(pieces)))


def head_block(u):
    return u // NB, NB - 1 - u % NB


class Causal:
    @staticmethod
    def width(u):
        return (head_block(u)[1] + 1) * P

    @staticmethod
    def count(u):
        return -(-Causal.width(u) // CW)

    @staticmethod
    def before(u):
        return sum(Causal.count(v) for v in range(u))


class Memory:
    @staticmethod
    def width(u):
        return MEM

    @staticmethod
    def count(u):
        return 1

    @staticmethod
    def before(u):
        return u


def spans(width):
    return [(c, min(c + CW, width)) for c in range(0, width, CW)]


def hybrid_layer(nc, x, mem, w_tiles, w_forget, w_out, norm_w, mem_norm_w, out_norm_w, b_forget,
                 final_norm_w, out):
    yT_dram = nc.dram_tensor("yT_dram", (NT_OUT, P, S), F32, kind="Internal").ap()
    negL_dram = nc.dram_tensor("negL_dram", (FH, S), F32, kind="Internal").ap()

    with ExitStack() as ctx:
        def sb(name, shape, dt=F32):
            return ctx.enter_context(nc.sbuf_tensor(name, shape, dt))

        def sem(name):
            return ctx.enter_context(nc.semaphore(name))

        hT = sb("hT", [P, 2, KT, S], F32R)
        sb_heads = sb("sb_heads", [P, 8 * S], F32R)
        fx_heads = sb("fx_heads", [P, 8 * S], F32R)
        w_raw = sb("w_raw", [P, KT * P])
        w_parts = sb("w_parts", [P, 2, 2, KT * P], F32R)
        pT = sb("pT", [P, 3, 2, CW], F32R)
        work = sb("work", [P, 6, S])
        negL = sb("negL", [P, 2, S])
        y = sb("y", [P, NB, 2, HD])
        silu = sb("silu", [P, 2, S])
        diag = sb("diag", [P, 2, P])
        o_tmp = sb("o_tmp", [P, 4, HD])
        ident = sb("ident", [P, P])
        out_g = sb("out_g", [P, NT_OUT])
        in_g = sb("in_g", [P, KT])
        mem_g = sb("mem_g", [P, KT])
        b_f = sb("b_f", [FH, 1])
        peak = sb("peak", [P, 4 * RING])
        npeak = sb("npeak", [P, 2 * UNITS])
        rowsum = sb("rowsum", [P, 2 * UNITS])
        rinv = sb("rinv", [P, 4])
        ssq = sb("ssq", [P, MPAIR, NB, 2])
        rs = sb("rs", [P, 3, 2 * UNITS])

        banks = ctx.enter_context(nc.psum_tensor("banks", [P, 8, CW], F32))
        S_BANK, T_BANK, O_BANK, PJ_BANK = 0, 3, 5, 6

        def q_of(region):
            return region[:, 0:2 * S].rearrange("p (h t) -> p h t", h=2)

        def k_of(region):
            return region[:, 2 * S:6 * S].rearrange("p (h l t) -> p h l t", h=2, l=2)

        def v_of(region):
            return region[:, 6 * S:8 * S].rearrange("p (b h c) -> p b h c", b=NB, h=2)

        def v_raw(c):
            return silu[:, 0, c * CW:(c + 1) * CW]

        mem_k = sb_heads[:, 0:2 * S].rearrange("p (h l t) -> p h l t", h=4, l=2)
        mem_q = sb_heads[:, 2 * S:6 * S].rearrange("p (h t) -> p h t", h=4)
        memT = sb_heads[:, 2 * S:6 * S].rearrange("p (l k t) -> p l k t", l=2, k=KT)
        mem_v = sb_heads[:, 6 * S:7 * S].rearrange("p (b h c) -> p b h c", b=MB, h=4)
        forget_hi = fx_heads[:, 0:KT * FH]
        forget_lo = fx_heads[:, KT * FH:2 * KT * FH]
        mem_rows = [work[:, RING + b, :] for b in range(MB)]
        y2 = work[:, RING, :].rearrange("p (b h c) -> p b h c", b=NB, h=2)
        y_of = [y[:, :, :, :], y2]
        hT_flat = hT[:, :, :, :].rearrange("p l k t -> p (l k t)")
        wo_at = [(fx_heads, 2 * D * j) for j in range(4)] + [(hT_flat, 2 * D * j) for j in range(NT_OUT - 4)]
        wo_hl = [r[:, a:a + 2 * D].rearrange("p (l n) -> p l n", l=2) for r, a in wo_at]
        wo_raw = [w_raw[:, :], work[:, RING + 1, :], work[:, RING + 2, :]]
        y_raw = [negL[:, b, :] for b in range(2)]
        YW = 2 * NPAIR * P
        y_at = 2 * D * (NT_OUT - 4)
        y_hl = [hT_flat[:, y_at + 2 * YW * b:y_at + 2 * YW * (b + 1)].rearrange("p (l j t) -> p l j t", l=2, j=2 * NPAIR)
                for b in range(2)]
        mem_hl = sb_heads[:, 4 * S:8 * S].rearrange("p (l j t) -> p l j t", l=2, j=MPAIR)
        res = [work[:, i, :] for i in range(RING)]
        final_g = y[:, :, :, :].rearrange("p a b c -> p (a b c)")
        squares = work[:, RING, :]

        consts_in, x_in, x_in2, w_in_dma, wf_in = sem("consts_in"), sem("x_in"), sem("x_in2"), sem("w_in_dma"), sem("wf_in")
        ident_zero, ident_done = sem("ident_zero"), sem("ident_done")
        x_ssq, x_rstd, x_scaled = sem("x_ssq"), sem("x_rstd"), sem("x_scaled")
        xT_ready, xT_hi, xT_lo = sem("xT_ready"), sem("xT_hi"), sem("xT_lo")
        wf_hi, wf_lo, f_logit = sem("wf_hi"), sem("wf_lo"), sem("f_logit")
        f_abs, f_exp, f_ln, f_scan, negL_out, negL_in = (sem("f_abs"), sem("f_exp"), sem("f_ln"), sem("f_scan"),
                                                         sem("negL_out"), sem("negL_in"))
        w_hi, w_lo = sem("w_hi"), sem("w_lo")
        piece_ready, piece_hi, piece_done, k_dup = sem("piece_ready"), sem("piece_hi"), sem("piece_done"), sem("k_dup")
        s_ready, sb_read, fx_read = sem("s_ready"), sem("sb_read"), sem("fx_read")
        fail_masked, beta_masked, scanned, sb_p = sem("fail_masked"), sem("beta_masked"), sem("scanned"), sem("sb_p")
        diag_ready, fx_max, fx_p = sem("diag_ready"), sem("fx_max"), sem("fx_p")
        t_ready, t_hi, t_lo, pv_done = sem("t_ready"), sem("t_hi"), sem("t_lo"), sem("pv_done")
        o_lo, o_read, o_done, y_ready, y_out = sem("o_lo"), sem("o_read"), sem("o_done"), sem("y_ready"), sem("y_out")
        gate_sig = sem("gate_sig")
        mem_in, mem_ssq, mem_rstd, mem_scaled, mem_evac = (sem("mem_in"), sem("mem_ssq"), sem("mem_rstd"),
                                                           sem("mem_scaled"), sem("mem_evac"))
        wo_in, wo_hi, wo_lo = [sem(f"wo_in{i}") for i in range(3)], sem("wo_hi"), sem("wo_lo")
        yb_in, xb_in, fin_in = [sem("yb_in0"), sem("yb_in1")], [sem(f"xb_in{i}") for i in range(RING)], sem("fin_in")
        my_hi, my_lo = sem("my_hi"), sem("my_lo")
        yb_hi, yb_lo, proj_out, res_sum, res_ssq, res_done = (sem("yb_hi"), sem("yb_lo"), sem("proj_out"), sem("res_sum"),
                                                              sem("res_ssq"), sem("res_done"))
        stored = [sem(f"stored{i}") for i in range(RING)]
        dve_step = sem("dve_step")

        def tile_no(kind, it, j):
            if kind == "sb":
                return it * TURN_TILES + (FIRST_TILES + j)
            if kind == "fx":
                return it * TURN_TILES + (FIRST_TILES + 5 + j)
            return MEM_TILE0 + j
        SB_N, LAST_N = 14, 16

        def piece_no(kind, it, q):
            if kind == "sb":
                return it * TURN_PIECES + (FIRST_PIECES + q)
            if kind in ("fx", "last"):
                return it * TURN_PIECES + (FIRST_PIECES + SB_N + q)
            return FIRST_PIECES + (NPAIR - 1) * TURN_PIECES + SB_N + LAST_N + q

        def hi_no(kind, it, q):
            turn, n = TURN_PIECES - 2 * 4, sum(p[0] != "V" for p in PIECES[kind][:q])
            if kind == "sb":
                return it * turn + (FIRST_PIECES - 2 + n)
            if kind in ("fx", "last"):
                return it * turn + (FIRST_PIECES - 2 + SB_N - 4 + n)
            return FIRST_PIECES - 2 + (NPAIR - 1) * turn + SB_N - 4 + LAST_N - 2 + n

        def bank_of(kind, it, q):
            return PJ_BANK + q % 2

        def chunk_no(kind, it, g):
            return it * 48 + g if kind == "sb" else it * 48 + (24 + g) if kind != "mm" else 48 * NPAIR + g

        group_no = chunk_no

        def unit_no(kind, it, u):
            return it * UNITS + u if kind != "mm" else NPAIR * UNITS + u

        def half_no(kind, it, h):
            return it * 8 + h if kind == "sb" else it * 8 + (4 + h) if kind != "mm" else 8 * NPAIR + h

        def pair_no(kind, it):
            return it * 2 if kind == "sb" else it * 2 + 1 if kind != "mm" else 2 * NPAIR

        def out_tile(kind, it, pair):
            return it if kind == "sb" else it + NPAIR if kind != "mm" else 2 * NPAIR + pair

        def side_of(kind, pair):
            return 0 if kind == "sb" else 1 if kind != "mm" else pair

        def pairs_of(kind):
            return MPAIR if kind == "mm" else 1

        def geometry(kind):
            return Memory if kind == "mm" else Causal

        def tile_parity(kind, it, j):
            if kind == "sb":
                return (FIRST_TILES + j) % 2
            if kind == "fx":
                return (FIRST_TILES + 5 + j) % 2
            return tile_no(kind, it, j) % 2

        def region_of(kind):
            return sb_heads if kind == "sb" else fx_heads

        def target_of(kind):
            return fx_heads if kind == "sb" else sb_heads

        def closes_tile(piece):
            return piece[1] is not None and (piece[0] in ("memK", "memV") or piece[2] == 1)

        def wait_alone(eng, what, value):
            value = value if isinstance(value, int) else eng.to_reg(value)
            eng.wait_ge(consts_in, 64)
            eng.wait_ge(what, value)

        block = ctx.enter_context(nc.Block())

        @block.sync
        def _(sp):
            def wait(what, value):
                wait_alone(sp, what, value)

            def load_tile(n):
                wait(w_hi, n)
                wait(w_lo, n)
                sp.dma_start(w_raw[:, :], w_tiles[bass.ds(n, 1), :, :]).then_inc(w_in_dma, 16)

            def copy_keys(region, n_piece):
                wait(piece_done, n_piece + 1)
                k = k_of(region)
                sp.dma_start(k[HD:P, 0, :, :].bitcast(F32), k[0:HD, 0, :, :].bitcast(F32)).then_inc(k_dup, 16)
                sp.dma_start(k[0:HD, 1, :, :].bitcast(F32), k[HD:P, 1, :, :].bitcast(F32)).then_inc(k_dup, 16)

            def phase(kind, it):
                pieces = PIECES[kind]
                if kind == "sb":
                    for h in range(2):
                        sp.dma_start(negL[:, h, :], negL_dram[bass.ds(it * 2 + h, 1), :].broadcast_to((P, S))
                                     ).then_inc(negL_in, 16)
                tiles = 0
                for q, piece in enumerate(pieces):
                    if piece[0] == "memT" and piece[2] == 0:
                        for b in range(MB):
                            sp.dma_start(mem_rows[b], mem[0, b * P:(b + 1) * P, :]).then_inc(mem_in, 16)
                    if closes_tile(piece):
                        n = tile_no(kind, it, piece[1])
                        if kind in ("sb", "fx") or n + 3 < N_TILES:
                            load_tile(n + 3)
                        if piece[0] == "K":
                            copy_keys(target_of(kind), piece_no(kind, it, q))
                        tiles += 1
                        if tiles == 1 and kind in ("fx", "last"):
                            wait(y_out, (it * 2 + 1) * 16)
                if kind == "last":
                    for m, h in ((0, 0), (0, 1), (1, 2), (1, 3)):
                        mine, other = (slice(0, HD), slice(HD, P)) if h % 2 == 0 else (slice(HD, P), slice(0, HD))
                        wait(piece_done, piece_no(kind, it, 4 + m) + 1)
                        sp.dma_start(mem_k[other, h, :, :].bitcast(F32), mem_k[mine, h, :, :].bitcast(F32)).then_inc(k_dup, 16)
                wait(piece_done, piece_no(kind, it, len(pieces) + 1) + 1)
                sp.dma_start(yT_dram[bass.ds(out_tile(kind, it, 0), 1), :, :], silu[:, side_of(kind, 0), :]).then_inc(y_out, 16)
                if kind in ("fx", "last"):
                    wait(y_out, (it * 2 + 2) * 16)

            def load_w_out(j):
                if j >= 3:
                    sp.wait_ge(wo_hi, j - 2)
                    sp.wait_ge(wo_lo, j - 2)
                sp.dma_start(wo_raw[j % 3], w_out[j * P:(j + 1) * P, :]).then_inc(wo_in[j % 3], 16)

            def load_y(m):
                if m >= 2:
                    sp.wait_ge(yb_lo, m - 1)
                sp.dma_start(y_raw[m % 2].rearrange("p (j t) -> p j t", j=2 * NPAIR),
                             yT_dram[0:2 * NPAIR, :, m * P:(m + 1) * P].rearrange("j p t -> p j t")).then_inc(yb_in[m % 2], 16)

            def load_x(m):
                if m >= RING:
                    sp.wait_ge(stored[m % RING], 16 * (m // RING))
                sp.dma_start(res[m % RING], x[0, m * P:(m + 1) * P, :]).then_inc(xb_in[m % RING], 16)

            for dst, src in ((in_g, norm_w), (mem_g, mem_norm_w), (out_g, out_norm_w), (b_f, b_forget)):
                sp.dma_start(dst[:, :], src).then_inc(consts_in, 16)
            for b in range(4):
                sp.dma_start(work[:, b, :], x[0, b * P:(b + 1) * P, :]).then_inc(x_in, 16)
            sp.dma_start(w_raw[:, :], w_tiles[0, :, :]).then_inc(w_in_dma, 16)
            sp.dma_start(diag[:, 0, 0:KT * FH], w_forget).then_inc(wf_in, 16)
            load_tile(1)
            sp.wait_ge(xT_ready, KT)
            for b in range(4):
                sp.dma_start(work[:, b, :], x[0, (4 + b) * P:(5 + b) * P, :]).then_inc(x_in2, 16)
            load_tile(2)
            load_tile(3)
            load_tile(4)
            copy_keys(sb_heads, 1)
            load_tile(5)
            sp.wait_ge(f_scan, 1)
            sp.dma_start(negL_dram[:, :], work[0:FH, 5, :]).then_inc(negL_out, 16)
            sp.wait_ge(negL_out, 16)
            with sp.Fori(0, NPAIR - 1) as it:
                phase("sb", it)
                phase("fx", it)
            phase("sb", NPAIR - 1)
            phase("last", NPAIR - 1)
            sp.wait_ge(w_hi, N_TILES)
            sp.wait_ge(w_lo, N_TILES)
            for j in range(3):
                load_w_out(j)
            for m in range(2):
                load_y(m)
            for j in range(3, NT_OUT):
                load_w_out(j)
            load_y(2)
            sp.wait_ge(piece_done, piece_no("mm", 0, len(PIECES["mm"]) + 2 * MPAIR))
            sp.dma_start(final_g, final_norm_w.broadcast_to((P, D))).then_inc(fin_in, 16)
            for m in range(RING):
                load_x(m)
            for m in range(NB):
                if m + 3 < NB:
                    load_y(m + 3)
                sp.wait_ge(res_done, m + 1)
                sp.dma_start(out[0, m * P:(m + 1) * P, :], res[m % RING]).then_inc(stored[m % RING], 16)
                if m + RING < NB:
                    load_x(m + RING)
            for b in range(RING):
                sp.wait_ge(stored[b], 16 * len(range(b, NB, RING)))

        @block.tensor
        def _(pe):
            def project(n, parity, c, bank):
                w = w_parts[:, parity, :, :].rearrange("p l (k c) -> p l k c", k=KT)
                pe.wait_ge(w_lo, n + 1)
                tok = slice(c * CW, (c + 1) * CW)
                for k in range(KT):
                    o = banks[:, bank, :]
                    pe.matmul(o, w[:, 0, k, :], hT[:, 0, k, tok], start=(k == 0), stop=False)
                    pe.matmul(o, w[:, 0, k, :], hT[:, 1, k, tok], start=False, stop=False)
                    mm = pe.matmul(o, w[:, 1, k, :], hT[:, 0, k, tok], start=False, stop=(k == KT - 1))
                    if k == KT - 1:
                        mm.then_inc(piece_ready, 1)
                    yield

            def transpose_values(c, bank):
                for b in range(4):
                    mm = pe.transpose(banks[:, bank, b * P:(b + 1) * P], v_raw(c)[:, b * P:(b + 1) * P], ident[:, :])
                mm.then_inc(piece_ready, 1)

            def parts_of(kind, it):
                pieces = PIECES[kind]
                for q, (what, tile, c, parts) in enumerate(pieces):
                    bank = bank_of(kind, it, q)
                    pe.wait_ge(piece_done, piece_no(kind, it, q) - 1)
                    if tile is not None:
                        parity = tile_parity(kind, it, tile)
                        n = tile_no(kind, it, tile)
                        w = w_parts[:, parity, :, :].rearrange("p l (k c) -> p l k c", k=KT)
                    if what == "VT":
                        pe.wait_ge(piece_done, piece_no(kind, it, q) - 1)
                        transpose_values(c, bank)
                        yield
                    elif what == "memT":
                        pe.wait_ge(mem_scaled, MB)
                        for i in range(4):
                            k, b = 2 * c + i // 2, i % 2
                            mm = pe.transpose(banks[:, bank, i * P:(i + 1) * P], mem_rows[b][:, k * P:(k + 1) * P], ident[:, :])
                        mm.then_inc(piece_ready, 1)
                        yield
                    elif what == "memK":
                        pe.wait_ge(w_lo, n + 1)
                        pe.wait_ge(piece_done, piece_no(kind, it, 4))
                        for k in range(KT):
                            o = banks[:, bank, 0:MEM]
                            pe.matmul(o, w[:, 0, k, :], memT[:, 0, k, :], start=(k == 0), stop=False)
                            pe.matmul(o, w[:, 0, k, :], memT[:, 1, k, :], start=False, stop=False)
                            mm = pe.matmul(o, w[:, 1, k, :], memT[:, 0, k, :], start=False, stop=(k == KT - 1))
                            if k == KT - 1:
                                mm.then_inc(piece_ready, 1)
                            if k % 2:
                                yield
                    elif what == "memV":
                        pe.wait_ge(w_lo, n + 1)
                        for b in range(MB):
                            tok = slice(b * P, (b + 1) * P)
                            for k in range(KT):
                                o = banks[:, bank, b * P:(b + 1) * P]
                                pe.matmul(o, memT[:, 0, k, tok], w[:, 0, k, :], start=(k == 0), stop=False)
                                pe.matmul(o, memT[:, 0, k, tok], w[:, 1, k, :], start=False, stop=False)
                                mm = pe.matmul(o, memT[:, 1, k, tok], w[:, 0, k, :], start=False, stop=(k == KT - 1))
                                if b == MB - 1 and k == KT - 1:
                                    mm.then_inc(piece_ready, 1)
                                if k % 4 == 3:
                                    yield
                    else:
                        yield from project(n, parity, c, bank)

            def scores(kind, it, u):
                h, tb = head_block(u)
                geo = geometry(kind)
                q0 = slice(tb * P, (tb + 1) * P)
                if kind == "mm":
                    q = mem_q[:, h, q0]
                    k = mem_k[:, h, :, :]
                else:
                    q = q_of(region_of(kind))[:, h, q0]
                    k = k_of(region_of(kind))[:, h, :, :]
                for i, (c0, c1) in enumerate(spans(geo.width(u))):
                    g = geo.before(u) + i
                    if g >= 3:
                        if kind == "sb":
                            pe.wait_ge(sb_read, it * 24 + (g - 2))
                        elif kind == "mm":
                            pe.wait_ge(fx_p, unit_no(kind, it, g) - 2)
                        else:
                            pe.wait_ge(fx_read, it * 24 + (g - 2))
                    o = banks[:, S_BANK + g % 3, 0:c1 - c0]
                    pe.matmul(o, q, k[:, 0, c0:c1], start=True, stop=False)
                    pe.matmul(o, q, k[:, 1, c0:c1], start=False, stop=True).then_inc(s_ready, 1)

            def transposes(kind, it, u):
                h, tb = head_block(u)
                geo = geometry(kind)
                n_sb = geo.width(u) // P
                if kind == "sb":
                    pe.wait_ge(sb_p, unit_no(kind, it, u) + 1)
                    p = work[:, RING + u % RING, :]
                else:
                    pe.wait_ge(fx_p, unit_no(kind, it, u) + 1)
                    p = work[:, u % RING, :]
                for i in range((n_sb + 3) // 4):
                    g = geo.before(u) + i
                    if g >= 2:
                        pe.wait_ge(t_lo, group_no(kind, it, g) - 1)
                    for s in range(4 * i, min(4 * i + 4, n_sb)):
                        mm = pe.transpose(banks[:, T_BANK + g % 2, (s - 4 * i) * P:(s - 4 * i + 1) * P],
                                          p[:, s * P:(s + 1) * P], ident[:, :])
                    mm.then_inc(t_ready, 1)

            def values(kind, it, u):
                h, tb = head_block(u)
                geo = geometry(kind)
                n_sb = geo.width(u) // P
                v = mem_v[:, :, h, :] if kind == "mm" else v_of(region_of(kind))[:, :, h, :]
                half = u // 4
                if u == 0 and kind in ("sb", "fx", "last"):
                    pe.wait_ge(piece_done, it * TURN_PIECES + (FIRST_PIECES + (0 if kind == "sb" else 8)))
                if u % 4 == 0 and half:
                    pe.wait_ge(o_read, half_no(kind, it, half))
                o = (tb % 4) * P
                for i in range((n_sb + 3) // 4):
                    g = geo.before(u) + i
                    pe.wait_ge(t_lo, group_no(kind, it, g) + 1)
                    for s in range(4 * i, min(4 * i + 4, n_sb)):
                        part = pT[:, g % 3, :, (s - 4 * i) * P:(s - 4 * i + 1) * P]
                        pe.matmul(banks[:, O_BANK, o:o + P], part[:, 0, :], v[:, s, :], start=(s == 0), stop=(s == n_sb - 1))
                        mm = pe.matmul(banks[:, O_BANK, o:o + HD], part[:, 1, :], v[:, s, 0:HD], start=False,
                                       stop=(s == n_sb - 1), skip_group_check=True)
                    mm.then_inc(pv_done, 1)

            def head(kind, it):
                if kind == "sb":
                    pe.wait_ge(piece_done, it * TURN_PIECES + (FIRST_PIECES - 6))
                    pe.wait_ge(k_dup, it * 64 + 32)
                elif kind == "mm":
                    pe.wait_ge(k_dup, NPAIR * 64 + 64)
                    pe.wait_ge(piece_done, piece_no("last", NPAIR - 1, 12))
                else:
                    pe.wait_ge(k_dup, it * 64 + 64)
                    pe.wait_ge(piece_done, it * TURN_PIECES + (FIRST_PIECES + 4))
                for i in range(HEAD):
                    scores(kind, it, i)

            def phase(kind, it, following=None):
                pieces = PIECES[kind]
                issue, done, last = plan(kind)
                work_left = parts_of(kind, it)
                for i in range(HEAD, STEPS[kind]):
                    if i < N_UNITS[kind]:
                        scores(kind, it, i)
                    for _ in range(issue[i]):
                        next(work_left)
                    if T_LAG <= i < N_UNITS[kind] + T_LAG:
                        transposes(kind, it, i - T_LAG)
                    if PV_LAG <= i:
                        values(kind, it, i - PV_LAG)
                if following:
                    head(*following)
                for _ in work_left:
                    pass
                if kind == "mm":
                    project_out(0, range(2 * NPAIR))
                pe.wait_ge(y_ready, pair_no(kind, it) + 1)
                for c in range(2 * pairs_of(kind)):
                    q = len(pieces) + c
                    pe.wait_ge(piece_done, piece_no(kind, it, q) - 1)
                    for b in range(4):
                        mm = pe.transpose(banks[:, bank_of(kind, it, q), b * P:(b + 1) * P],
                                          y_of[c // 2][:, 4 * (c % 2) + b, :, :].rearrange("p h c -> p (h c)"), ident[:, :])
                    mm.then_inc(piece_ready, 1)

            def project_out(m, tiles):
                b = m % 2
                if tiles[0] == 0:
                    pe.wait_ge(yb_lo, m + 1)
                    if m >= 2:
                        pe.wait_ge(res_sum, m - 1)
                elif m == 0:
                    pe.wait_ge(my_lo, 2 * MPAIR)
                for j in tiles:
                    if m == 0:
                        pe.wait_ge(wo_lo, j + 1)
                    for l, r in ((0, 0), (0, 1), (1, 0)):
                        yt = y_hl[b][:, l, j, :] if j < 2 * NPAIR else mem_hl[:, l, j - 2 * NPAIR, m * P:(m + 1) * P]
                        for c in range(2):
                            mm = pe.matmul(banks[:, 2 * b + c, :], yt, wo_hl[j][:, r, c * CW:(c + 1) * CW],
                                           start=(j == 0 and (l, r) == (0, 0)), stop=(j == NT_OUT - 1 and l == 1))
                if tiles[-1] == NT_OUT - 1:
                    mm.then_inc(proj_out, 1)

            pe.wait_ge(ident_done, 1)
            for c in range(2):
                pe.wait_ge(x_scaled, 4 * (c + 1))
                for k in range(KT):
                    g = c * KT + k
                    if g >= 2:
                        pe.wait_ge(xT_lo, g - 1)
                    for b in range(4):
                        mm = pe.transpose(banks[:, T_BANK + g % 2, b * P:(b + 1) * P], work[:, b, k * P:(k + 1) * P], ident[:, :])
                    mm.then_inc(xT_ready, 1)
            pe.wait_ge(xT_lo, 2 * KT)
            pe.wait_ge(wf_lo, 1)
            for c in range(2):
                tok = slice(c * CW, (c + 1) * CW)
                for k in range(KT):
                    f = slice(k * FH, (k + 1) * FH)
                    o = banks[0:FH, S_BANK + c, :]
                    pe.matmul(o, forget_hi[:, f], hT[:, 0, k, tok], start=(k == 0), stop=False)
                    pe.matmul(o, forget_hi[:, f], hT[:, 1, k, tok], start=False, stop=False)
                    mm = pe.matmul(o, forget_lo[:, f], hT[:, 0, k, tok], start=False, stop=(k == KT - 1))
                mm.then_inc(f_logit, 1)
            for q, (what, tile, c, _) in enumerate(QKV_PIECES):
                if q >= 2:
                    pe.wait_ge(piece_done, q - 1)
                if what == "VT":
                    transpose_values(c, PJ_BANK + q % 2)
                else:
                    for _ in project(tile, tile % 2, c, PJ_BANK + q % 2):
                        pass
            pe.wait_ge(negL_out, 16)
            head("sb", 0)
            with pe.Fori(0, NPAIR - 1) as it:
                phase("sb", it, ("fx", it))
                phase("fx", it, ("sb", it + 1))
            phase("sb", NPAIR - 1, ("last", NPAIR - 1))
            phase("last", NPAIR - 1, ("mm", 0))
            phase("mm", 0)
            project_out(1, range(2 * NPAIR))
            for m in range(NB):
                if m >= 2:
                    project_out(m, range(2 * NPAIR))
                project_out(m, range(2 * NPAIR, NT_OUT))

        @block.scalar
        def _(act):
            def split_hi(n, parity):
                act.wait_ge(w_in_dma, (n + 1) * 16)
                act.activation(w_parts[:, parity, 0, :], w_raw[:, :], ACT.Copy).then_inc(w_hi, 1)

            def evacuate(kind, it, piece, q_no, bank):
                what, tile, c, _ = piece
                act.wait_ge(piece_ready, q_no + 1)
                if what == "V":
                    return
                src = banks[:, bank, :]
                cols = slice(c * CW, (c + 1) * CW)
                if what == "Q":
                    q = q_of(target_of(kind))
                    act.activation(q[0:HD, 0, cols], src[0:HD], ACT.Copy, scale=SCALE)
                    ins = act.activation(q[HD:P, 1, cols], src[HD:P], ACT.Copy, scale=SCALE)
                elif what == "K":
                    k = k_of(target_of(kind))
                    act.activation(k[0:HD, 0, 0, cols], src[0:HD], ACT.Copy)
                    ins = act.activation(k[HD:P, 1, 0, cols], src[HD:P], ACT.Copy)
                elif what == "VT":
                    ins = act.activation(v_of(target_of(kind))[:, 4 * c:4 * c + 4, :, 0:HD],
                                         src.rearrange("p (b h c) -> p b h c", b=4, h=2), ACT.Copy)
                elif what in ("G0", "G1", "memG0", "memG1"):
                    if what in ("memG0", "memG1"):
                        act.wait_ge(y_out, 16 * (2 * NPAIR - 1 + int(what[-1])))
                    ins = act.activation(silu[:, int(what[-1]), cols], src, ACT.Sigmoid)
                elif what == "memT":
                    for i in range(2):
                        k = 2 * c + i
                        ins = act.activation(memT[:, 0, k, :], src[:, i * MEM:(i + 1) * MEM], ACT.Copy, scale=mem_g[:, k:k + 1])
                elif what == "memK":
                    act.activation(mem_k[0:HD, 2 * c, 0, :], src[0:HD, 0:MEM], ACT.Copy)
                    ins = act.activation(mem_k[HD:P, 2 * c + 1, 0, :], src[HD:P, 0:MEM], ACT.Copy)
                elif what == "memV":
                    for b in range(MB):
                        ins = act.activation(mem_v[:, b, 2 * c:2 * c + 2, 0:HD],
                                             src[:, b * P:(b + 1) * P].rearrange("p (h c) -> p h c", h=2), ACT.Copy)
                elif what in ("memQ0", "memQ1"):
                    h = 2 * int(what[-1])
                    act.activation(mem_q[0:HD, h, cols], src[0:HD], ACT.Copy, scale=SCALE)
                    ins = act.activation(mem_q[HD:P, h + 1, cols], src[HD:P], ACT.Copy, scale=SCALE)
                ins.then_inc(piece_hi, 1)

            def evacuate_and_split(kind, it, q):
                pieces = PIECES[kind]
                evacuate(kind, it, pieces[q], piece_no(kind, it, q), bank_of(kind, it, q))
                if closes_tile(pieces[q]):
                    n = tile_no(kind, it, pieces[q][1])
                    if kind in ("sb", "fx") or n + 2 < N_TILES:
                        split_hi(n + 2, tile_parity(kind, it, pieces[q][1]))

            def sigmoids(it, u):
                h, tb = head_block(u)
                if u >= RING:
                    act.wait_ge(t_ready, it * 48 + Causal.before(u - RING + 1))
                for i, (c0, c1) in enumerate(spans(Causal.width(u))):
                    g = Causal.before(u) + i
                    act.wait_ge(s_ready, chunk_no("sb", it, g) + 1)
                    src = banks[:, S_BANK + g % 3, 0:c1 - c0]
                    act.activation(work[:, u % RING, c0:c1], src, ACT.Sigmoid, scale=-1.0)
                    act.activation(work[:, RING + u % RING, c0:c1], src, ACT.Sigmoid).then_inc(sb_read, 1)

            def exponentials(kind, it, u):
                act.wait_ge(fx_max, unit_no(kind, it, u) + 1)
                h, tb = head_block(u)
                p = work[:, u % RING, 0:geometry(kind).width(u)]
                if kind == "mm":
                    if u >= RING:
                        act.wait_ge(t_ready, group_no(kind, it, u - RING) + 1)
                    act.activation(p, banks[:, S_BANK + u % 3, 0:MEM], ACT.Exp, bias=npeak[:, u:u + 1],
                                   accum_out=rowsum[:, h * NB + tb:h * NB + tb + 1]).then_inc(fx_p, 1)
                else:
                    act.activation(p, p, ACT.Exp, bias=npeak[:, u:u + 1], accum_out=rowsum[:, h * NB + tb:h * NB + tb + 1]).then_inc(fx_p, 1)

            def upper_parts(kind, it, u):
                geo = geometry(kind)
                n_sb = geo.width(u) // P
                for i in range((n_sb + 3) // 4):
                    g = geo.before(u) + i
                    n = min(4, n_sb - 4 * i) * P
                    act.wait_ge(t_ready, group_no(kind, it, g) + 1)
                    if g >= 3:
                        act.wait_ge(pv_done, group_no(kind, it, g) - 2)
                    act.activation(pT[:, g % 3, 0, 0:n], banks[:, T_BANK + g % 2, 0:n],
                                   ACT.Copy).then_inc(t_hi, 1)

            def output_lo(kind, it, half):
                geo = geometry(kind)
                act.wait_ge(pv_done, group_no(kind, it, geo.before(4 * half + 4)))
                if half:
                    act.wait_ge(o_done, half_no(kind, it, half))
                act.activation(o_tmp[:, :, :], banks[:, O_BANK, :].rearrange("p (b c) -> p b c", b=4)[:, :, HD:P],
                               ACT.Copy).then_inc(o_lo, 1)

            def mem_norm(stage):
                if stage == 0:
                    act.wait_ge(mem_in, 16 * MB)
                    for b in range(MB):
                        act.activation(work[:, RING + 2, :], mem_rows[b], ACT.Square, accum_out=rs[:, 2, b:b + 1]).then_inc(mem_ssq, 1)
                        act.wait_ge(mem_ssq, b + 1)
                else:
                    act.wait_ge(mem_rstd, 1)
                    for b in range(MB):
                        act.activation(mem_rows[b], mem_rows[b], ACT.Copy, scale=rs[:, 1, b:b + 1]).then_inc(mem_scaled, 1)

            def w_out_hi(j):
                act.wait_ge(wo_in[j % 3], 16 * (j // 3 + 1))
                act.activation(wo_hl[j][:, 0, :], wo_raw[j % 3], ACT.Copy).then_inc(wo_hi, 1)

            def y_hi(m):
                act.wait_ge(yb_in[m % 2], 16 * (m // 2 + 1))
                if m >= 2:
                    act.wait_ge(proj_out, m - 1)
                act.activation(y_hl[m % 2][:, 0, :, :], y_raw[m % 2].rearrange("p (j t) -> p j t", j=2 * NPAIR),
                               ACT.Copy).then_inc(yb_hi, 1)

            def first_parts(kind, it, i):
                if kind == "sb":
                    if i < N_UNITS[kind]:
                        sigmoids(it, i)
                elif 0 <= i - EXP_LAG < N_UNITS[kind]:
                    exponentials(kind, it, i - EXP_LAG)

            def head(kind, it):
                for i in range(HEAD):
                    first_parts(kind, it, i)

            def phase(kind, it, following=None):
                pieces = PIECES[kind]
                issue, done, last = plan(kind)
                for i in range(HEAD, STEPS[kind]):
                    first_parts(kind, it, i)
                    if kind == "last" and MEM_STEP <= i < MEM_STEP + 2:
                        mem_norm(i - MEM_STEP)
                    if kind == "mm" and i in WO_STEP:
                        w_out_hi(WO_STEP[i])
                    if kind == "mm" and i in Y_STEP:
                        y_hi(Y_STEP[i])
                    for q in done[i]:
                        evacuate_and_split(kind, it, q)
                    if T_LAG <= i < N_UNITS[kind] + T_LAG:
                        upper_parts(kind, it, i - T_LAG)
                    if PV_LAG <= i and (i - PV_LAG) % 4 == 3:
                        output_lo(kind, it, (i - PV_LAG) // 4)
                if following:
                    head(*following)
                for q in last:
                    evacuate_and_split(kind, it, q)

            act.wait_ge(w_in_dma, 16)
            act.activation(w_parts[:, 0, 0, :], w_raw[:, :], ACT.Copy).then_inc(w_hi, 1)
            for b in range(NB):
                if b < 4:
                    act.wait_ge(x_in, 64)
                else:
                    act.wait_ge(x_in2, 64)
                act.activation(work[:, 4, :], work[:, b % 4, :], ACT.Square, accum_out=ssq[:, 0, b, 0:1]).then_inc(x_ssq, 1)
                act.wait_ge(x_ssq, b + 1)
                if b % 4 == 3:
                    act.wait_ge(x_rstd, b // 4 + 1)
                    for i in range(4):
                        act.activation(work[:, i, :], work[:, i, :], ACT.Copy, scale=rs[:, 1, b - 3 + i:b - 2 + i]).then_inc(x_scaled, 1)
                    act.wait_ge(consts_in, 64)
                    for k in range(KT):
                        g = (b // 4) * KT + k
                        act.wait_ge(xT_ready, g + 1)
                        act.activation(hT[:, 0, k, (b // 4) * CW:(b // 4 + 1) * CW], banks[:, T_BANK + g % 2, :], ACT.Copy,
                                       scale=in_g[:, k:k + 1]).then_inc(xT_hi, 1)
                if b == 3:
                    split_hi(1, 1)
                    act.wait_ge(wf_in, 16)
                    act.activation(forget_hi, diag[:, 0, 0:KT * FH], ACT.Copy).then_inc(wf_hi, 1)
            act.wait_ge(f_abs, 1)
            act.activation(work[0:FH, 2, :], work[0:FH, 1, :], ACT.Exp, scale=-1.0).then_inc(f_exp, 1)
            act.wait_ge(f_exp, 1)
            act.activation(work[0:FH, 3, :], work[0:FH, 2, :], ACT.Ln, bias=1.0).then_inc(f_ln, 1)
            for q, piece in enumerate(QKV_PIECES):
                evacuate("fx", 0, piece, q, PJ_BANK + q % 2)
                if closes_tile(piece):
                    split_hi(piece[1] + 2, piece[1] % 2)
            head("sb", 0)
            with act.Fori(0, NPAIR - 1) as it:
                phase("sb", it, ("fx", it))
                phase("fx", it, ("sb", it + 1))
            phase("sb", NPAIR - 1, ("last", NPAIR - 1))
            phase("last", NPAIR - 1, ("mm", 0))
            phase("mm", 0)
            for c in range(2 * MPAIR):
                act.wait_ge(piece_done, piece_no("mm", 0, len(PIECES["mm"]) + c) + 1)
                cols = slice(c % 2 * CW, (c % 2 + 1) * CW)
                act.activation(mem_hl[:, 0, c // 2, cols], silu[:, c // 2, cols], ACT.Copy).then_inc(my_hi, 1)
            for m in range(NB):
                if m + 2 < NB:
                    y_hi(m + 2)
                act.wait_ge(res_sum, m + 1)
                if m:
                    act.wait_ge(res_ssq, m)
                act.activation(squares, res[m % RING], ACT.Square, accum_out=rs[:, 2, 0:1]).then_inc(res_ssq, 1)

        @block.gpsimd
        def _(pool):
            fill_one, fill_zero, fill_lowest = pool.to_reg(1.0), pool.to_reg(0.0), pool.to_reg(LOWEST)

            def split_lo(n, parity):
                pool.wait_ge(w_hi, n + 1)
                pool.tensor_tensor(w_parts[:, parity, 1, :], w_raw[:, :], w_parts[:, parity, 0, :].bitcast(F32),
                                   ALU.subtract).then_inc(w_lo, 1)

            def masks(it, u):
                h, tb = head_block(u)
                wait_alone(pool, sb_read, it * 24 + Causal.before(u + 1))
                blk = slice(tb * P, (tb + 1) * P)
                f, b = work[:, u % RING, blk], work[:, RING + u % RING, blk]
                pool.affine_select(out=f, in_=f, compare_op=ALU.is_gt, fill=fill_one, base=0, pattern=[[-1, P]],
                                   channel_multiplier=1).then_inc(fail_masked, 1)
                pool.affine_select(out=b, in_=b, compare_op=ALU.is_gt, fill=fill_zero, base=0, pattern=[[-1, P]],
                                   channel_multiplier=1).then_inc(beta_masked, 1)

            def diagonal(kind, it, u):
                h, tb = head_block(u)
                if u >= 2:
                    wait_alone(pool, fx_read, it * 24 + Causal.before(u - 1))
                pool.affine_select(out=diag[:, u % 2, :], in_=negL[:, h, tb * P:(tb + 1) * P], compare_op=ALU.is_ge,
                                   fill=fill_lowest, base=0, pattern=[[-1, P]], channel_multiplier=1).then_inc(diag_ready, 1)

            def maybe_split(kind, it, q):
                pieces = PIECES[kind]
                if closes_tile(pieces[q]):
                    n = tile_no(kind, it, pieces[q][1])
                    if kind in ("sb", "fx") or n + 2 < N_TILES:
                        split_lo(n + 2, tile_parity(kind, it, pieces[q][1]))

            def head(kind, it):
                if kind in ("fx", "last"):
                    wait_alone(pool, negL_in, it * 32 + 32)
                for i in range(HEAD):
                    mask(kind, it, i)

            def mask(kind, it, i):
                if kind == "sb" and i < UNITS:
                    masks(it, i)
                elif kind in ("fx", "last") and i < UNITS:
                    diagonal(kind, it, i)

            def phase(kind, it, following=None):
                issue, done, last = plan(kind)
                for i in range(HEAD, STEPS[kind]):
                    mask(kind, it, i)
                    for q in done[i]:
                        maybe_split(kind, it, q)
                if following:
                    head(*following)
                for q in last:
                    maybe_split(kind, it, q)

            pool.memset(ident[:, :], 0.0).then_inc(ident_zero, 1)
            pool.wait_ge(ident_zero, 1)
            pool.affine_select(out=ident[:, :], in_=ident[:, :], compare_op=ALU.not_equal, fill=1.0, base=0,
                               pattern=[[-1, P]], channel_multiplier=1).then_inc(ident_done, 1)
            split_lo(0, 0)
            split_lo(1, 1)
            pool.wait_ge(wf_hi, 1)
            pool.tensor_tensor(forget_lo, diag[:, 0, 0:KT * FH], forget_hi.bitcast(F32), ALU.subtract).then_inc(wf_lo, 1)
            for t in range(FIRST_TILES):
                split_lo(t + 2, t % 2)
            head("sb", 0)
            with pool.Fori(0, NPAIR - 1) as it:
                phase("sb", it, ("fx", it))
                phase("fx", it, ("sb", it + 1))
            phase("sb", NPAIR - 1, ("last", NPAIR - 1))
            phase("last", NPAIR - 1, ("mm", 0))
            phase("mm", 0)
            for j in range(NT_OUT):
                pool.wait_ge(wo_hi, j + 1)
                pool.tensor_tensor(wo_hl[j][:, 1, :], wo_raw[j % 3], wo_hl[j][:, 0, :].bitcast(F32), ALU.subtract).then_inc(wo_lo, 1)

        @block.vector
        def _(dve):
            steps = {"base": 0, "n": 0}

            def link(ins):
                steps["n"] += 1
                ins.then_inc(dve_step, 1)
                dve.wait_ge(dve_step, steps["base"] + steps["n"])

            def rsqrt(v, n, mean, last=None):
                r, half, t = rs[:, 0, 0:n], rs[:, 2, 0:n], rs[:, 1, 0:n]
                link(dve.tensor_scalar(half, v, 1.0 / mean, EPS, ALU.mult, ALU.add))
                link(dve.tensor_scalar(t.bitcast(I32), half.bitcast(I32), 1, None, ALU.logical_shift_right))
                link(dve.tensor_scalar(r.bitcast(I32), t.bitcast(I32), -1.0, float(0x5F3759DF), ALU.mult, ALU.add))
                link(dve.tensor_scalar(half, half, -0.5, None, ALU.mult))
                for _ in range(4):
                    link(dve.tensor_tensor(t, r, r, ALU.mult))
                    link(dve.tensor_tensor(t, t, half, ALU.mult))
                    link(dve.scalar_tensor_tensor(out=r, in0=t, scalar=1.5, in1=r, op0=ALU.add, op1=ALU.mult))

            def evacuate(kind, piece, number, n_hi, bank, sent=None):
                what, tile, c, _ = piece
                src = banks[:, bank, :]
                if what == "V":
                    dve.wait_ge(piece_ready, number + 1)
                    if sent is not None:
                        dve.wait_ge(y_out, sent)
                    dve.tensor_copy(v_raw(c), src).then_inc(piece_done, 1)
                    return
                dve.wait_ge(piece_hi, n_hi + 1)
                cols = slice(c * CW, (c + 1) * CW)

                def scaled(dst, s, hi):
                    return dve.scalar_tensor_tensor(out=dst, in0=s, scalar=SCALE, in1=hi.bitcast(F32), op0=ALU.mult, op1=ALU.subtract)

                if what == "Q":
                    q = q_of(target_of(kind))
                    scaled(q[HD:P, 0, cols], src[0:HD], q[0:HD, 0, cols])
                    ins = scaled(q[0:HD, 1, cols], src[HD:P], q[HD:P, 1, cols])
                elif what == "K":
                    k = k_of(target_of(kind))
                    dve.tensor_tensor(k[0:HD, 0, 1, cols], src[0:HD], k[0:HD, 0, 0, cols].bitcast(F32), ALU.subtract)
                    ins = dve.tensor_tensor(k[HD:P, 1, 1, cols], src[HD:P], k[HD:P, 1, 0, cols].bitcast(F32), ALU.subtract)
                elif what == "VT":
                    v = v_of(target_of(kind))[:, 4 * c:4 * c + 4, :, :]
                    ins = dve.tensor_tensor(v[:, :, :, HD:P], src.rearrange("p (b h c) -> p b h c", b=4, h=2),
                                            v[:, :, :, 0:HD].bitcast(F32), ALU.subtract)
                elif what in ("G0", "G1", "memG0", "memG1"):
                    g = silu[:, int(what[-1]), cols]
                    ins = dve.tensor_tensor(g, src, g, ALU.mult)
                elif what == "memT":
                    for i in range(2):
                        k = 2 * c + i
                        ins = dve.scalar_tensor_tensor(out=memT[:, 1, k, :], in0=src[:, i * MEM:(i + 1) * MEM],
                                                       scalar=mem_g[:, k:k + 1], in1=memT[:, 0, k, :].bitcast(F32),
                                                       op0=ALU.mult, op1=ALU.subtract)
                elif what == "memK":
                    dve.tensor_tensor(mem_k[0:HD, 2 * c, 1, :], src[0:HD, 0:MEM], mem_k[0:HD, 2 * c, 0, :].bitcast(F32), ALU.subtract)
                    ins = dve.tensor_tensor(mem_k[HD:P, 2 * c + 1, 1, :], src[HD:P, 0:MEM],
                                            mem_k[HD:P, 2 * c + 1, 0, :].bitcast(F32), ALU.subtract)
                elif what == "memV":
                    for b in range(MB):
                        v = mem_v[:, b, 2 * c:2 * c + 2, :]
                        ins = dve.tensor_tensor(v[:, :, HD:P], src[:, b * P:(b + 1) * P].rearrange("p (h c) -> p h c", h=2),
                                                v[:, :, 0:HD].bitcast(F32), ALU.subtract)
                elif what in ("memQ0", "memQ1"):
                    h = 2 * int(what[-1])
                    scaled(mem_q[HD:P, h, cols], src[0:HD], mem_q[0:HD, h, cols])
                    ins = scaled(mem_q[0:HD, h + 1, cols], src[HD:P], mem_q[HD:P, h + 1, cols])
                ins.then_inc(piece_done, 1)

            def stick(kind, it, u):
                w = Causal.width(u)
                f, b = work[:, u % RING, :], work[:, RING + u % RING, :]
                dve.wait_ge(fail_masked, it * UNITS + (u + 1))
                left = f[:, w - 1:0:-1]
                dve.tensor_tensor_scan(left, left, left, 1.0, ALU.mult, ALU.bypass).then_inc(scanned, 1)
                dve.wait_ge(beta_masked, it * UNITS + (u + 1))
                dve.wait_ge(scanned, it * UNITS + (u + 1))
                dve.tensor_tensor(b[:, 0:w - 1], b[:, 0:w - 1], f[:, 1:w], ALU.mult).then_inc(sb_p, 1)

            def logits(kind, it, u):
                h, tb = head_block(u)
                if u >= RING:
                    dve.wait_ge(t_ready, group_no(kind, it, Causal.before(u - RING + 1)))
                dve.wait_ge(diag_ready, it * UNITS + (u + 1))
                start, n = LOWEST, 4 * (u % RING)
                for i, (c0, c1) in enumerate(spans(Causal.width(u))):
                    g = Causal.before(u) + i
                    wait_alone(dve, s_ready, chunk_no(kind, it, g) + 1)
                    cuts = [(a, b) for a, b in ((c0, min(c1, tb * P)), (max(c0, tb * P), c1)) if a < b]
                    for a, b in cuts:
                        bias = diag[:, u % 2, :] if a == tb * P else negL[:, h, a:b]
                        ins = dve.tensor_tensor_reduce(out=work[:, u % RING, a:b], in0=banks[:, S_BANK + g % 3, a - c0:b - c0],
                                                       in1=bias, scale=1.0, scalar=start, op0=ALU.add, op1=ALU.max,
                                                       accum_out=peak[:, n:n + 1])
                        start, n = peak[:, n:n + 1], n + 1
                        if b == c1:
                            ins.then_inc(fx_read, 1)
                            wait_alone(dve, fx_read, it * 24 + (g + 1))
                        else:
                            steps["n"] += 1
                            ins.then_inc(dve_step, 1)
                            wait_alone(dve, dve_step, steps["base"] + steps["n"])
                dve.tensor_scalar(npeak[:, u:u + 1], start, -1.0, None, ALU.mult).then_inc(fx_max, 1)

            def mem_max(kind, it, u):
                dve.wait_ge(s_ready, chunk_no(kind, it, u) + 1)
                top = peak[:, 4 * (u % RING):4 * (u % RING) + 1]
                link(dve.reduce_max(top, banks[:, S_BANK + u % 3, 0:MEM], AX_X))
                dve.tensor_scalar(npeak[:, u:u + 1], top, -1.0, None, ALU.mult).then_inc(fx_max, 1)

            def rows(kind, it, u):
                (stick if kind == "sb" else mem_max if kind == "mm" else logits)(kind, it, u)

            def head(kind, it):
                for u in range(HEAD):
                    rows(kind, it, u)

            def phase(kind, it, following=None):
                pieces = PIECES[kind]
                issue, done, last = plan(kind)
                geo = geometry(kind)

                def piece(q):
                    evacuate(kind, pieces[q], piece_no(kind, it, q), hi_no(kind, it, q), bank_of(kind, it, q),
                             it * 32 + 16 if kind == "fx" else None)

                def lower_parts(u):
                    n_sb = geo.width(u) // P
                    for i in range((n_sb + 3) // 4):
                        g = geo.before(u) + i
                        n = min(4, n_sb - 4 * i) * P
                        dve.wait_ge(t_hi, group_no(kind, it, g) + 1)
                        part = pT[:, g % 3, :, 0:n]
                        dve.tensor_tensor(part[:, 1, :], banks[:, T_BANK + g % 2, 0:n], part[:, 0, :].bitcast(F32),
                                          ALU.subtract).then_inc(t_lo, 1)

                def output(half):
                    pair, h, b0 = half // 4, half // 2 % 2, 4 * (1 - half % 2)
                    o = y_of[pair][:, b0:b0 + 4, h, :]
                    dve.wait_ge(o_lo, half_no(kind, it, half) + 1)
                    dve.tensor_tensor(o, banks[:, O_BANK, :].rearrange("p (b c) -> p b c", b=4)[:, :, 0:HD], o_tmp[:, :, :],
                                      ALU.add).then_inc(o_read, 1)
                    dve.wait_ge(o_read, half_no(kind, it, half) + 1)
                    if kind != "sb":
                        sums = rowsum[:, half // 2 * NB + b0:half // 2 * NB + b0 + 4]
                        link(dve.reciprocal(rinv[:, :], sums))
                        link(dve.tensor_tensor(o, o, rinv[:, :].unsqueeze(2).broadcast_to((P, 4, HD)), ALU.mult))
                    link(dve.tensor_tensor(o_tmp[:, :, :], o, o, ALU.mult))
                    dve.reduce_sum(ssq[:, pair, b0:b0 + 4, h], o_tmp[:, :, :], AX_X).then_inc(o_done, 1)

                for i in range(HEAD, STEPS[kind]):
                    if i < N_UNITS[kind] and kind != "sb":
                        rows(kind, it, i)
                    if kind == "last" and i == MEM_STEP + 1:
                        dve.wait_ge(mem_ssq, MB)
                        rsqrt(rs[:, 2, 0:MB], MB, D)
                        dve.tensor_copy(rs[:, 1, 0:MB], rs[:, 0, 0:MB]).then_inc(mem_rstd, 1)
                    for q in done[i]:
                        piece(q)
                    if T_LAG <= i < N_UNITS[kind] + T_LAG:
                        lower_parts(i - T_LAG)
                    if i < N_UNITS[kind] and kind == "sb":
                        rows(kind, it, i)
                    if kind == "mm" and i in Y_STEP:
                        y_lo(Y_STEP[i])
                    if PV_LAG <= i and (i - PV_LAG) % 4 == 3:
                        output((i - PV_LAG) // 4)
                if following and following[0] != "sb":
                    rows(*following, 0)
                n_pairs = pairs_of(kind)
                dve.wait_ge(o_done, half_no(kind, it, N_UNITS[kind] // 4 - 1) + 1)
                rsqrt(ssq[:, 0:n_pairs, :, :].rearrange("p a b h -> p (a b h)"), UNITS * n_pairs, HD)
                for pair in range(n_pairs):
                    yv = y_of[pair].rearrange("p b h c -> p (b h) c")
                    r = rs[:, 0, UNITS * pair:UNITS * (pair + 1)]
                    ins = dve.tensor_tensor(yv, yv, r.unsqueeze(2).broadcast_to((P, UNITS, HD)), ALU.mult)
                ins.then_inc(y_ready, 1)
                if following and following[0] == "sb":
                    rows(*following, 0)
                    piece(last[0])
                    last = last[1:]
                if following:
                    rows(*following, 1)
                for q in last:
                    piece(q)
                for c in range(2 * n_pairs):
                    q = len(pieces) + c
                    dve.wait_ge(piece_ready, piece_no(kind, it, q) + 1)
                    g = silu[:, side_of(kind, c // 2), c % 2 * CW:(c % 2 + 1) * CW]
                    t = out_tile(kind, it, c // 2)
                    dve.scalar_tensor_tensor(out=g, in0=banks[:, bank_of(kind, it, q), :], scalar=out_g[:, bass.ds(t, 1)], in1=g,
                                             op0=ALU.mult, op1=ALU.mult).then_inc(piece_done, 1)

            def y_lo(m):
                dve.wait_ge(yb_hi, m + 1)
                dve.tensor_tensor(y_hl[m % 2][:, 1, :, :], y_raw[m % 2].rearrange("p (j t) -> p j t", j=2 * NPAIR),
                                  y_hl[m % 2][:, 0, :, :].bitcast(F32), ALU.subtract).then_inc(yb_lo, 1)

            for c in range(2):
                dve.wait_ge(x_ssq, 4 * (c + 1))
                if c:
                    dve.wait_ge(x_scaled, 4)
                rsqrt(ssq[:, 0, 4 * c:4 * c + 4, 0], 4, D)
                dve.tensor_copy(rs[:, 1, 4 * c:4 * c + 4], rs[:, 0, 0:4]).then_inc(x_rstd, 1)
                if c == 0:
                    dve.wait_ge(consts_in, 64)
                for k in range(KT):
                    g = c * KT + k
                    dve.wait_ge(xT_hi, g + 1)
                    cols = slice(c * CW, (c + 1) * CW)
                    dve.scalar_tensor_tensor(out=hT[:, 1, k, cols], in0=banks[:, T_BANK + g % 2, :], scalar=in_g[:, k:k + 1],
                                             in1=hT[:, 0, k, cols].bitcast(F32), op0=ALU.mult, op1=ALU.subtract).then_inc(xT_lo, 1)
            u, a, m, one, cum = (work[0:FH, i, :] for i in (0, 1, 4, 2, 5))
            dve.wait_ge(f_logit, 2)
            for c in range(2):
                link(dve.tensor_scalar(u[:, c * CW:(c + 1) * CW], banks[0:FH, S_BANK + c, :], b_f[:, 0:1], None, ALU.add))
            dve.scalar_tensor_tensor(out=a, in0=u, scalar=-1.0, in1=u, op0=ALU.mult, op1=ALU.max).then_inc(f_abs, 1)
            link(dve.tensor_scalar(m, u, -1.0, 0.0, ALU.mult, ALU.max))
            dve.wait_ge(f_ln, 1)
            link(dve.tensor_tensor(m, m, work[0:FH, 3, :], ALU.add))
            link(dve.memset(one, 1.0))
            dve.tensor_tensor_scan(cum, one, m, 0.0, ALU.mult, ALU.add).then_inc(f_scan, 1)
            for q, piece in enumerate(QKV_PIECES):
                evacuate("fx", piece, q, sum(p[0] != "V" for p in QKV_PIECES[:q]), PJ_BANK + q % 2)
            before_loop = steps["n"]
            head("sb", 0)
            with dve.Fori(0, NPAIR - 1) as it:
                steps["base"], steps["n"] = it * TURN_STEPS + before_loop, 0
                phase("sb", it, ("fx", it))
                phase("fx", it, ("sb", it + 1))
                assert steps["n"] == TURN_STEPS, steps["n"]
            steps["base"], steps["n"] = before_loop + (NPAIR - 1) * TURN_STEPS, 0
            phase("sb", NPAIR - 1, ("last", NPAIR - 1))
            phase("last", NPAIR - 1, ("mm", 0))
            phase("mm", 0)
            for c in range(2 * MPAIR):
                dve.wait_ge(my_hi, c + 1)
                cols = slice(c % 2 * CW, (c % 2 + 1) * CW)
                dve.tensor_tensor(mem_hl[:, 1, c // 2, cols], silu[:, c // 2, cols], mem_hl[:, 0, c // 2, cols].bitcast(F32),
                                  ALU.subtract).then_inc(my_lo, 1)
            dve.wait_ge(fin_in, 16)
            for m in range(NB):
                b = m % 2
                r = res[m % RING]
                dve.wait_ge(proj_out, m + 1)
                dve.wait_ge(xb_in[m % RING], 16 * (m // RING + 1))
                dve.tensor_tensor(r, banks[:, 2 * b:2 * b + 2, :].rearrange("p b c -> p (b c)"), r, ALU.add).then_inc(res_sum, 1)
                if m + 2 < NB:
                    y_lo(m + 2)
                dve.wait_ge(res_ssq, m + 1)
                rsqrt(rs[:, 2, 0:1], 1, D)
                dve.scalar_tensor_tensor(out=r, in0=r, scalar=rs[:, 0, 0:1], in1=final_g, op0=ALU.mult,
                                         op1=ALU.mult).then_inc(res_done, 1)


def kernel(x, mem, norm_w, w_in, b_forget, mem_norm_w, w_mem_kv, out_norm_w, w_out, final_norm_w):
    import numpy as np
    import concourse.bacc as bacc
    from concourse import mybir as mb
    from concourse.bass_utils import run_bass_kernel_spmd

    def tiles(w, starts):
        w = np.asarray(w)
        return [w[:, s:s + P].reshape(KT, P, P).transpose(1, 0, 2).reshape(P, KT * P) for s in starts]

    w = np.asarray(w_in)[0]
    sbw, gate0, mq0, f0 = 512, 3336, 3080, 3072
    qkv = lambda base, pair: [base + i * sbw + pair * P for i in (1, 0, 2)]
    order = []
    for it in range(NPAIR):
        if it == 0:
            order += qkv(0, 0)
        order += qkv(3 * sbw, it) + [gate0 + it * P, gate0 + (NPAIR + it) * P]
        if it < NPAIR - 1:
            order += qkv(0, it + 1)
    w_tiles = tiles(w, order) + tiles(np.asarray(w_mem_kv)[0], [0, P, 2 * P, 3 * P])
    w_tiles += tiles(w, [mq0, mq0 + P, gate0 + 2 * NPAIR * P, gate0 + (2 * NPAIR + 1) * P])
    w_forget = w[:, f0:f0 + FH].reshape(KT, P, FH).transpose(1, 0, 2).reshape(P, KT * FH)
    arrays = {
        "in_x": np.asarray(x), "in_mem": np.asarray(mem), "in_w_tiles": np.stack(w_tiles), "in_w_forget": w_forget,
        "in_w_out": np.asarray(w_out)[0], "in_norm_w": np.asarray(norm_w).reshape(KT, P).T,
        "in_mem_norm_w": np.asarray(mem_norm_w).reshape(KT, P).T, "in_out_norm_w": np.asarray(out_norm_w).reshape(NT_OUT, P).T,
        "in_b_forget": np.asarray(b_forget).reshape(FH, 1), "in_final_norm_w": np.asarray(final_norm_w).reshape(1, D),
    }
    arrays = {k: np.ascontiguousarray(v) for k, v in arrays.items()}
    nc = bacc.Bacc("TRN2", target_bir_lowering=False, num_devices=1)
    args = [nc.dram_tensor(k, v.shape, mb.dt.from_np(v.dtype), kind="ExternalInput").ap() for k, v in arrays.items()]
    args.append(nc.dram_tensor("out_y", (1, S, D), F32, kind="ExternalOutput").ap())
    hybrid_layer(nc, *args)
    r = run_bass_kernel_spmd(nc, [arrays], core_ids=[0])
    return r.results[0]["out_y"]
```

```python
from contextlib import ExitStack

import concourse.bass as bass
from concourse import mybir

ALU = mybir.AluOpType
ACT = mybir.ActivationFunctionType
AX_X = mybir.AxisListType.X
F32 = mybir.dt.float32
F32R = mybir.dt.float32r
I32 = mybir.dt.int32

P = 128
D = 1024
S = 1024
KT = D // P
NB = S // P
HD = 64
NPAIR = 4
MPAIR = 2
MEM = 256
MB = MEM // P
NT_OUT = 2 * NPAIR + MPAIR
FH = 8
CW = 512
EPS = 1e-6
SCALE = HD ** -0.5
LOWEST = -3.0e38

UNITS = 2 * NB
EXP_LAG = 1
T_LAG = 2
PV_LAG = {"sb": 3, "fx": 3, "last": 3, "mm": 4}
RING = 3
LIGHT = 2.0
HEAD = 2

FIRST_TILES = 3
TURN_TILES = 8
MEM_TILE0 = FIRST_TILES + TURN_TILES * (NPAIR - 1) + 5
N_TILES = MEM_TILE0 + 2 * MPAIR + 2 * MPAIR
FIRST_PIECES = 2 * FIRST_TILES + 2
TURN_PIECES = 24
RSQRT_STEPS = 4 + 3 * 3
TURN_STEPS = 2 * RSQRT_STEPS + 4 * 1 + 4 * 3 + 2 * 6


def tile_pieces(what, tile):
    return [(what, tile, 0, 8), (what, tile, 1, 8)]


QKV_PIECES = tile_pieces("K", 0) + tile_pieces("Q", 1) + tile_pieces("V", 2) + [("VT", None, 0, 1), ("VT", None, 1, 1)]
FIRST_ORDER = [("K", 0, 0, 8), ("Q", 1, 0, 8), ("K", 0, 1, 8), ("Q", 1, 1, 8)] + QKV_PIECES[4:]
SB_PIECES = QKV_PIECES + tile_pieces("G0", 3) + tile_pieces("G1", 4)
FX_PIECES = QKV_PIECES
LAST_PIECES = ([("memT", None, g, 1) for g in range(4)]
               + [("memK", 0, 0, 4), ("memK", 1, 1, 4), ("memV", 2, 0, 4), ("memV", 3, 1, 4)]
               + tile_pieces("memQ0", 4) + tile_pieces("memQ1", 5) + tile_pieces("memG0", 6))
PIECES = {"sb": SB_PIECES, "fx": FX_PIECES, "last": LAST_PIECES, "mm": tile_pieces("memG1", 7)}
TAIL = {"sb": 1, "fx": 3, "last": 1, "mm": 0}
N_UNITS = {"sb": UNITS, "fx": UNITS, "last": UNITS, "mm": 2 * UNITS}
STEPS = {k: n + PV_LAG[k] for k, n in N_UNITS.items()}
MEM_STEP = 4
ACTIVE = {"sb": (HEAD, STEPS["sb"]), "fx": (HEAD, STEPS["fx"]), "last": (MEM_STEP + 2, UNITS + 1), "mm": (HEAD, 24)}
WO_STEP = {2: 0, 4: 1, 6: 2, 9: 3, 25: 4, 26: 5, 28: 6, 30: 7, 32: 8, 34: 9}
Y_STEP = {24: 0, 27: 1}


def plan(kind):
    pieces, tail = PIECES[kind], TAIL[kind]
    n_steps = STEPS[kind]
    inside = pieces[:len(pieces) - tail]
    total = sum(p[3] for p in inside)
    ends, at = [], 0
    for p in inside:
        at += p[3]
        ends.append(at)
    first, behind = ACTIVE[kind]
    def weight(s):
        if not first <= s < behind:
            return 0
        return 1 if kind == "mm" else LIGHT - Causal.width(s) / S if s < UNITS else LIGHT
    weights = [weight(s) for s in range(n_steps)]
    issued = [round(total * sum(weights[:s + 1]) / sum(weights)) for s in range(n_steps)]
    parts = [issued[s] - (issued[s - 1] if s else 0) for s in range(n_steps)]
    done = [[q for q, e in enumerate(ends) if (issued[s - 1] if s else 0) < e <= issued[s]] for s in range(n_steps)]
    return parts, done, list(range(len(inside), len(pieces)))


def head_block(u, kind=None):
    if kind == "mm":
        return u // NB, u % NB
    v = u // 2
    return (0, v) if u % 2 == 0 else (1, NB - 2 - 2 * (v // 2) + v % 2)


def early_row(kind, step):
    row = step - (STEPS[kind] - HEAD)
    return row if row >= 0 else None


class Causal:
    @staticmethod
    def width(u):
        return (head_block(u)[1] + 1) * P

    @staticmethod
    def count(u):
        return -(-Causal.width(u) // CW)

    @staticmethod
    def before(u):
        return sum(Causal.count(v) for v in range(u))


class Memory:
    @staticmethod
    def width(u):
        return MEM

    @staticmethod
    def count(u):
        return 1

    @staticmethod
    def before(u):
        return u


def spans(width):
    return [(c, min(c + CW, width)) for c in range(0, width, CW)]


def hybrid_layer(nc, x, mem, w_tiles, w_forget, w_out, norm_w, mem_norm_w, out_norm_w, b_forget,
                 final_norm_w, out):
    yT_dram = nc.dram_tensor("yT_dram", (NT_OUT, P, S), F32, kind="Internal").ap()
    negL_dram = nc.dram_tensor("negL_dram", (FH, S), F32, kind="Internal").ap()

    with ExitStack() as ctx:
        def sb(name, shape, dt=F32):
            return ctx.enter_context(nc.sbuf_tensor(name, shape, dt))

        def sem(name):
            return ctx.enter_context(nc.semaphore(name))

        hT = sb("hT", [P, 2, KT, S], F32R)
        sb_heads = sb("sb_heads", [P, 8 * S], F32R)
        fx_heads = sb("fx_heads", [P, 8 * S], F32R)
        w_raw = sb("w_raw", [P, KT * P])
        w_parts = sb("w_parts", [P, 2, 2, KT * P], F32R)
        pT = sb("pT", [P, 3, 2, CW], F32R)
        work = sb("work", [P, 6, S])
        negL = sb("negL", [P, 2, S])
        y = sb("y", [P, NB, 2, HD])
        silu = sb("silu", [P, 2, S])
        diag = sb("diag", [P, 2, P])
        o_tmp = sb("o_tmp", [P, 4, HD])
        ident = sb("ident", [P, P])
        out_g = sb("out_g", [P, NT_OUT])
        in_g = sb("in_g", [P, KT])
        mem_g = sb("mem_g", [P, KT])
        b_f = sb("b_f", [FH, 1])
        peak = sb("peak", [P, 4 * RING])
        npeak = sb("npeak", [P, 2 * UNITS])
        rowsum = sb("rowsum", [P, 2 * UNITS])
        rinv = sb("rinv", [P, 4])
        ssq = sb("ssq", [P, MPAIR, NB, 2])
        rs = sb("rs", [P, 3, 2 * UNITS])

        banks = ctx.enter_context(nc.psum_tensor("banks", [P, 8, CW], F32))
        S_BANK, T_BANK, O_BANK, PJ_BANK = 0, 3, 5, 6

        def q_of(region):
            return region[:, 0:2 * S].rearrange("p (h t) -> p h t", h=2)

        def k_of(region):
            return region[:, 2 * S:6 * S].rearrange("p (h l t) -> p h l t", h=2, l=2)

        def v_of(region):
            return region[:, 6 * S:8 * S].rearrange("p (b h c) -> p b h c", b=NB, h=2)

        def v_raw(c):
            return silu[:, 0, c * CW:(c + 1) * CW]

        mem_k = sb_heads[:, 0:2 * S].rearrange("p (h l t) -> p h l t", h=4, l=2)
        mem_q = sb_heads[:, 2 * S:6 * S].rearrange("p (h t) -> p h t", h=4)
        memT = sb_heads[:, 2 * S:6 * S].rearrange("p (l k t) -> p l k t", l=2, k=KT)
        mem_v = sb_heads[:, 6 * S:7 * S].rearrange("p (b h c) -> p b h c", b=MB, h=4)
        forget_hi = fx_heads[:, 0:KT * FH]
        forget_lo = fx_heads[:, KT * FH:2 * KT * FH]
        mem_rows = [work[:, RING + b, :] for b in range(MB)]
        y2 = work[:, RING, :].rearrange("p (b h c) -> p b h c", b=NB, h=2)
        y_of = [y[:, :, :, :], y2]
        hT_flat = hT[:, :, :, :].rearrange("p l k t -> p (l k t)")
        wo_at = [(fx_heads, 2 * D * j) for j in range(4)] + [(hT_flat, 2 * D * j) for j in range(NT_OUT - 4)]
        wo_hl = [r[:, a:a + 2 * D].rearrange("p (l n) -> p l n", l=2) for r, a in wo_at]
        wo_raw = [w_raw[:, :], work[:, RING + 1, :], work[:, RING + 2, :]]
        y_raw = [negL[:, b, :] for b in range(2)]
        YW = 2 * NPAIR * P
        y_at = 2 * D * (NT_OUT - 4)
        y_hl = [hT_flat[:, y_at + 2 * YW * b:y_at + 2 * YW * (b + 1)].rearrange("p (l j t) -> p l j t", l=2, j=2 * NPAIR)
                for b in range(2)]
        mem_hl = sb_heads[:, 4 * S:8 * S].rearrange("p (l j t) -> p l j t", l=2, j=MPAIR)
        x_rows = [work[:, i, :] for i in range(6)] + [silu[:, i, :] for i in range(2)]
        y_flat = y[:, :, :, :].rearrange("p a b c -> p (a b c)")
        f_u, f_a, f_m, f_one = work[0:FH, 2, :], y_flat[0:FH, :], silu[0:FH, 1, :], work[0:FH, 5, :]
        res = [work[:, i, :] for i in range(RING)]
        final_g = y_flat
        squares = work[:, RING, :]

        consts_in, w_in_dma, wf_in = sem("consts_in"), sem("w_in_dma"), sem("wf_in")
        x_in = [sem(f"x_in{b}") for b in range(NB)]
        ident_zero, ident_done = sem("ident_zero"), sem("ident_done")
        x_ssq, x_scaled = sem("x_ssq"), sem("x_scaled")
        xT_ready, xT_hi, xT_lo = sem("xT_ready"), sem("xT_hi"), sem("xT_lo")
        wf_hi, wf_lo, f_logit = sem("wf_hi"), sem("wf_lo"), sem("f_logit")
        f_abs, f_exp, f_ln, f_scan, negL_out, negL_in = (sem("f_abs"), sem("f_exp"), sem("f_ln"), sem("f_scan"),
                                                         sem("negL_out"), sem("negL_in"))
        w_hi, w_lo = sem("w_hi"), sem("w_lo")
        piece_ready, piece_hi, piece_done, k_dup = sem("piece_ready"), sem("piece_hi"), sem("piece_done"), sem("k_dup")
        s_ready, sb_read, fx_read = sem("s_ready"), sem("sb_read"), sem("fx_read")
        fail_masked, beta_masked, scanned, sb_p = sem("fail_masked"), sem("beta_masked"), sem("scanned"), sem("sb_p")
        diag_ready, fx_max, fx_p = sem("diag_ready"), sem("fx_max"), sem("fx_p")
        t_ready, t_hi, t_lo, pv_done = sem("t_ready"), sem("t_hi"), sem("t_lo"), sem("pv_done")
        o_lo, o_read, o_done, y_ready, y_out = sem("o_lo"), sem("o_read"), sem("o_done"), sem("y_ready"), sem("y_out")
        gate_sig = sem("gate_sig")
        mem_in, mem_ssq, mem_rstd, mem_scaled = sem("mem_in"), sem("mem_ssq"), sem("mem_rstd"), sem("mem_scaled")
        wo_in, wo_hi, wo_lo = [sem(f"wo_in{i}") for i in range(3)], sem("wo_hi"), sem("wo_lo")
        yb_in, xb_in, fin_in = [sem("yb_in0"), sem("yb_in1")], [sem(f"xb_in{i}") for i in range(RING)], sem("fin_in")
        my_hi, my_lo = sem("my_hi"), sem("my_lo")
        yb_hi, yb_lo, proj_out, res_sum, res_ssq, res_done = (sem("yb_hi"), sem("yb_lo"), sem("proj_out"), sem("res_sum"),
                                                              sem("res_ssq"), sem("res_done"))
        stored = [sem(f"stored{i}") for i in range(RING)]
        dve_step = sem("dve_step")

        def tile_no(kind, it, j):
            if kind == "sb":
                return it * TURN_TILES + (FIRST_TILES + j)
            if kind == "fx":
                return it * TURN_TILES + (FIRST_TILES + 5 + j)
            return MEM_TILE0 + j
        SB_N, LAST_N = 14, 16

        def piece_no(kind, it, q):
            if kind == "sb":
                return it * TURN_PIECES + (FIRST_PIECES + q)
            if kind in ("fx", "last"):
                return it * TURN_PIECES + (FIRST_PIECES + SB_N + q)
            return FIRST_PIECES + (NPAIR - 1) * TURN_PIECES + SB_N + LAST_N + q

        def hi_no(kind, it, q):
            turn, n = TURN_PIECES - 2 * 4, sum(p[0] != "V" for p in PIECES[kind][:q])
            if kind == "sb":
                return it * turn + (FIRST_PIECES - 2 + n)
            if kind in ("fx", "last"):
                return it * turn + (FIRST_PIECES - 2 + SB_N - 4 + n)
            return FIRST_PIECES - 2 + (NPAIR - 1) * turn + SB_N - 4 + LAST_N - 2 + n

        def bank_of(kind, it, q):
            return PJ_BANK + q % 2

        def chunk_no(kind, it, g):
            return it * 48 + g if kind == "sb" else it * 48 + (24 + g) if kind != "mm" else 48 * NPAIR + g

        group_no = chunk_no

        def unit_no(kind, it, u):
            return it * UNITS + u if kind != "mm" else NPAIR * UNITS + u

        def half_no(kind, it, h):
            return it * 8 + h if kind == "sb" else it * 8 + (4 + h) if kind != "mm" else 8 * NPAIR + h

        def pair_no(kind, it):
            return it * 2 if kind == "sb" else it * 2 + 1 if kind != "mm" else 2 * NPAIR

        def out_tile(kind, it, pair):
            return it if kind == "sb" else it + NPAIR if kind != "mm" else 2 * NPAIR + pair

        def side_of(kind, pair):
            return 0 if kind == "sb" else 1 if kind != "mm" else pair

        def pairs_of(kind):
            return MPAIR if kind == "mm" else 1

        def geometry(kind):
            return Memory if kind == "mm" else Causal

        def tile_parity(kind, it, j):
            if kind == "sb":
                return (FIRST_TILES + j) % 2
            if kind == "fx":
                return (FIRST_TILES + 5 + j) % 2
            return tile_no(kind, it, j) % 2

        def region_of(kind):
            return sb_heads if kind == "sb" else fx_heads

        def target_of(kind):
            return fx_heads if kind == "sb" else sb_heads

        def closes_tile(piece):
            return piece[1] is not None and (piece[0] in ("memK", "memV") or piece[2] == 1)

        def wait_alone(eng, what, value):
            value = value if isinstance(value, int) else eng.to_reg(value)
            eng.wait_ge(consts_in, 64)
            eng.wait_ge(what, value)

        block = ctx.enter_context(nc.Block())

        @block.sync
        def _(sp):
            def wait(what, value):
                wait_alone(sp, what, value)

            def load_tile(n):
                wait(w_hi, n)
                wait(w_lo, n)
                sp.dma_start(w_raw[:, :], w_tiles[bass.ds(n, 1), :, :]).then_inc(w_in_dma, 16)

            def copy_keys(region, n_piece):
                wait(piece_done, n_piece + 1)
                k = k_of(region)
                sp.dma_start(k[HD:P, 0, :, :].bitcast(F32), k[0:HD, 0, :, :].bitcast(F32)).then_inc(k_dup, 16)
                sp.dma_start(k[0:HD, 1, :, :].bitcast(F32), k[HD:P, 1, :, :].bitcast(F32)).then_inc(k_dup, 16)

            def phase(kind, it):
                pieces = PIECES[kind]
                if kind == "sb":
                    for h in range(2):
                        sp.dma_start(negL[:, h, :], negL_dram[bass.ds(it * 2 + h, 1), :].broadcast_to((P, S))
                                     ).then_inc(negL_in, 16)
                tiles = 0
                for q, piece in enumerate(pieces):
                    if piece[0] == "memT" and piece[2] == 0:
                        for b in range(MB):
                            sp.dma_start(mem_rows[b], mem[0, b * P:(b + 1) * P, :]).then_inc(mem_in, 16)
                    if closes_tile(piece):
                        n = tile_no(kind, it, piece[1])
                        if kind in ("sb", "fx") or n + 3 < N_TILES:
                            load_tile(n + 3)
                        if piece[0] == "K":
                            copy_keys(target_of(kind), piece_no(kind, it, q))
                        tiles += 1
                        if tiles == 1 and kind in ("fx", "last"):
                            wait(y_out, (it * 2 + 1) * 16)
                if kind == "last":
                    for m, h in ((0, 0), (0, 1), (1, 2), (1, 3)):
                        mine, other = (slice(0, HD), slice(HD, P)) if h % 2 == 0 else (slice(HD, P), slice(0, HD))
                        wait(piece_done, piece_no(kind, it, 4 + m) + 1)
                        sp.dma_start(mem_k[other, h, :, :].bitcast(F32), mem_k[mine, h, :, :].bitcast(F32)).then_inc(k_dup, 16)
                wait(piece_done, piece_no(kind, it, len(pieces) + 1) + 1)
                sp.dma_start(yT_dram[bass.ds(out_tile(kind, it, 0), 1), :, :], silu[:, side_of(kind, 0), :]).then_inc(y_out, 16)
                if kind in ("fx", "last"):
                    wait(y_out, (it * 2 + 2) * 16)

            def load_w_out(j):
                if j >= 3:
                    sp.wait_ge(wo_hi, j - 2)
                    sp.wait_ge(wo_lo, j - 2)
                sp.dma_start(wo_raw[j % 3], w_out[j * P:(j + 1) * P, :]).then_inc(wo_in[j % 3], 16)

            def load_y(m):
                if m >= 2:
                    sp.wait_ge(yb_lo, m - 1)
                sp.dma_start(y_raw[m % 2].rearrange("p (j t) -> p j t", j=2 * NPAIR),
                             yT_dram[0:2 * NPAIR, :, m * P:(m + 1) * P].rearrange("j p t -> p j t")).then_inc(yb_in[m % 2], 16)

            def load_x(m):
                if m >= RING:
                    sp.wait_ge(stored[m % RING], 16 * (m // RING))
                sp.dma_start(res[m % RING], x[0, m * P:(m + 1) * P, :]).then_inc(xb_in[m % RING], 16)

            for b in range(4):
                sp.dma_start(x_rows[b], x[0, b * P:(b + 1) * P, :]).then_inc(x_in[b], 16)
            sp.dma_start(w_raw[:, :], w_tiles[0, :, :]).then_inc(w_in_dma, 16)
            for dst, src in ((in_g, norm_w), (mem_g, mem_norm_w), (out_g, out_norm_w), (b_f, b_forget)):
                sp.dma_start(dst[:, :], src).then_inc(consts_in, 16)
            for b in range(4, NB):
                sp.dma_start(x_rows[b], x[0, b * P:(b + 1) * P, :]).then_inc(x_in[b], 16)
            sp.dma_start(diag[:, 0, 0:KT * FH], w_forget).then_inc(wf_in, 16)
            load_tile(1)
            load_tile(2)
            load_tile(3)
            copy_keys(sb_heads, 2)
            sp.wait_ge(f_scan, 1)
            sp.dma_start(negL_dram[:, :], f_m).then_inc(negL_out, 16)
            sp.wait_ge(negL_out, 16)
            load_tile(4)
            load_tile(5)
            with sp.Fori(0, NPAIR - 1) as it:
                phase("sb", it)
                phase("fx", it)
            phase("sb", NPAIR - 1)
            phase("last", NPAIR - 1)
            sp.wait_ge(w_hi, N_TILES)
            sp.wait_ge(w_lo, N_TILES)
            for j in range(3):
                load_w_out(j)
            for m in range(2):
                load_y(m)
            for j in range(3, NT_OUT):
                load_w_out(j)
            load_y(2)
            sp.wait_ge(piece_done, piece_no("mm", 0, len(PIECES["mm"]) + 2 * MPAIR))
            sp.dma_start(final_g, final_norm_w.broadcast_to((P, D))).then_inc(fin_in, 16)
            for m in range(RING):
                load_x(m)
            for m in range(NB):
                if m + 3 < NB:
                    load_y(m + 3)
                sp.wait_ge(res_done, m + 1)
                sp.dma_start(out[0, m * P:(m + 1) * P, :], res[m % RING]).then_inc(stored[m % RING], 16)
                if m + RING < NB:
                    load_x(m + RING)
            for b in range(RING):
                sp.wait_ge(stored[b], 16 * len(range(b, NB, RING)))

        @block.tensor
        def _(pe):
            def project(n, parity, c, bank):
                w = w_parts[:, parity, :, :].rearrange("p l (k c) -> p l k c", k=KT)
                pe.wait_ge(w_lo, n + 1)
                tok = slice(c * CW, (c + 1) * CW)
                for k in range(KT):
                    o = banks[:, bank, :]
                    pe.matmul(o, w[:, 0, k, :], hT[:, 0, k, tok], start=(k == 0), stop=False)
                    pe.matmul(o, w[:, 0, k, :], hT[:, 1, k, tok], start=False, stop=False)
                    mm = pe.matmul(o, w[:, 1, k, :], hT[:, 0, k, tok], start=False, stop=(k == KT - 1))
                    if k == KT - 1:
                        mm.then_inc(piece_ready, 1)
                    yield

            def transpose_values(c, bank):
                for b in range(4):
                    mm = pe.transpose(banks[:, bank, b * P:(b + 1) * P], v_raw(c)[:, b * P:(b + 1) * P], ident[:, :])
                mm.then_inc(piece_ready, 1)

            def parts_of(kind, it):
                pieces = PIECES[kind]
                for q, (what, tile, c, parts) in enumerate(pieces):
                    bank = bank_of(kind, it, q)
                    pe.wait_ge(piece_done, piece_no(kind, it, q) - 1)
                    if tile is not None:
                        parity = tile_parity(kind, it, tile)
                        n = tile_no(kind, it, tile)
                        w = w_parts[:, parity, :, :].rearrange("p l (k c) -> p l k c", k=KT)
                    if what == "VT":
                        pe.wait_ge(piece_done, piece_no(kind, it, q) - 1)
                        transpose_values(c, bank)
                        yield
                    elif what == "memT":
                        pe.wait_ge(mem_scaled, MB)
                        for i in range(4):
                            k, b = 2 * c + i // 2, i % 2
                            mm = pe.transpose(banks[:, bank, i * P:(i + 1) * P], mem_rows[b][:, k * P:(k + 1) * P], ident[:, :])
                        mm.then_inc(piece_ready, 1)
                        yield
                    elif what == "memK":
                        pe.wait_ge(w_lo, n + 1)
                        pe.wait_ge(piece_done, piece_no(kind, it, 4))
                        for k in range(KT):
                            o = banks[:, bank, 0:MEM]
                            pe.matmul(o, w[:, 0, k, :], memT[:, 0, k, :], start=(k == 0), stop=False)
                            pe.matmul(o, w[:, 0, k, :], memT[:, 1, k, :], start=False, stop=False)
                            mm = pe.matmul(o, w[:, 1, k, :], memT[:, 0, k, :], start=False, stop=(k == KT - 1))
                            if k == KT - 1:
                                mm.then_inc(piece_ready, 1)
                            if k % 2:
                                yield
                    elif what == "memV":
                        pe.wait_ge(w_lo, n + 1)
                        for b in range(MB):
                            tok = slice(b * P, (b + 1) * P)
                            for k in range(KT):
                                o = banks[:, bank, b * P:(b + 1) * P]
                                pe.matmul(o, memT[:, 0, k, tok], w[:, 0, k, :], start=(k == 0), stop=False)
                                pe.matmul(o, memT[:, 0, k, tok], w[:, 1, k, :], start=False, stop=False)
                                mm = pe.matmul(o, memT[:, 1, k, tok], w[:, 0, k, :], start=False, stop=(k == KT - 1))
                                if b == MB - 1 and k == KT - 1:
                                    mm.then_inc(piece_ready, 1)
                                if k % 4 == 3:
                                    yield
                    else:
                        yield from project(n, parity, c, bank)

            def scores(kind, it, u):
                h, tb = head_block(u, kind)
                geo = geometry(kind)
                q0 = slice(tb * P, (tb + 1) * P)
                if kind == "mm":
                    q = mem_q[:, h, q0]
                    k = mem_k[:, h, :, :]
                else:
                    q = q_of(region_of(kind))[:, h, q0]
                    k = k_of(region_of(kind))[:, h, :, :]
                for i, (c0, c1) in enumerate(spans(geo.width(u))):
                    g = geo.before(u) + i
                    if g >= 3:
                        if kind == "sb":
                            pe.wait_ge(sb_read, it * 24 + (g - 2))
                        elif kind == "mm":
                            pe.wait_ge(fx_p, unit_no(kind, it, g) - 2)
                        else:
                            pe.wait_ge(fx_read, it * 24 + (g - 2))
                    o = banks[:, S_BANK + g % 3, 0:c1 - c0]
                    pe.matmul(o, q, k[:, 0, c0:c1], start=True, stop=False)
                    pe.matmul(o, q, k[:, 1, c0:c1], start=False, stop=True).then_inc(s_ready, 1)

            def transposes(kind, it, u):
                h, tb = head_block(u, kind)
                geo = geometry(kind)
                n_sb = geo.width(u) // P
                if kind == "sb":
                    pe.wait_ge(sb_p, unit_no(kind, it, u) + 1)
                    p = work[:, RING + u % RING, :]
                else:
                    pe.wait_ge(fx_p, unit_no(kind, it, u) + 1)
                    p = work[:, u % RING, :]
                for i in range((n_sb + 3) // 4):
                    g = geo.before(u) + i
                    if g >= 2:
                        pe.wait_ge(t_lo, group_no(kind, it, g) - 1)
                    for s in range(4 * i, min(4 * i + 4, n_sb)):
                        mm = pe.transpose(banks[:, T_BANK + g % 2, (s - 4 * i) * P:(s - 4 * i + 1) * P],
                                          p[:, s * P:(s + 1) * P], ident[:, :])
                    mm.then_inc(t_ready, 1)

            def values(kind, it, u):
                h, tb = head_block(u, kind)
                geo = geometry(kind)
                n_sb = geo.width(u) // P
                v = mem_v[:, :, h, :] if kind == "mm" else v_of(region_of(kind))[:, :, h, :]
                half = u // 4
                if u == 0 and kind in ("sb", "fx", "last"):
                    pe.wait_ge(piece_done, it * TURN_PIECES + (FIRST_PIECES + (0 if kind == "sb" else 8)))
                if u % 4 == 0 and half:
                    pe.wait_ge(o_read, half_no(kind, it, half))
                o = (u % 4) * P
                for i in range((n_sb + 3) // 4):
                    g = geo.before(u) + i
                    pe.wait_ge(t_lo, group_no(kind, it, g) + 1)
                    for s in range(4 * i, min(4 * i + 4, n_sb)):
                        part = pT[:, g % 3, :, (s - 4 * i) * P:(s - 4 * i + 1) * P]
                        pe.matmul(banks[:, O_BANK, o:o + P], part[:, 0, :], v[:, s, :], start=(s == 0), stop=(s == n_sb - 1))
                        mm = pe.matmul(banks[:, O_BANK, o:o + HD], part[:, 1, :], v[:, s, 0:HD], start=False,
                                       stop=(s == n_sb - 1), skip_group_check=True)
                    mm.then_inc(pv_done, 1)

            def first_scores(kind, it, i):
                if i:
                    scores(kind, it, i)
                    return
                if kind == "sb":
                    pe.wait_ge(piece_done, it * TURN_PIECES + (FIRST_PIECES - 6))
                    pe.wait_ge(k_dup, it * 64 + 32)
                elif kind == "mm":
                    pe.wait_ge(k_dup, NPAIR * 64 + 64)
                    pe.wait_ge(piece_done, piece_no("last", NPAIR - 1, 12))
                else:
                    pe.wait_ge(k_dup, it * 64 + 64)
                    pe.wait_ge(piece_done, it * TURN_PIECES + (FIRST_PIECES + 4))
                scores(kind, it, i)

            def head(kind, it):
                for i in range(HEAD):
                    first_scores(kind, it, i)

            def phase(kind, it, following=None):
                pieces = PIECES[kind]
                issue, done, last = plan(kind)
                work_left = parts_of(kind, it)
                for i in range(HEAD, STEPS[kind]):
                    if i < N_UNITS[kind]:
                        scores(kind, it, i)
                    elif following and early_row(kind, i) is not None:
                        first_scores(*following, early_row(kind, i))
                    for _ in range(issue[i]):
                        next(work_left)
                    if T_LAG <= i < N_UNITS[kind] + T_LAG:
                        transposes(kind, it, i - T_LAG)
                    if PV_LAG[kind] <= i:
                        values(kind, it, i - PV_LAG[kind])
                for _ in work_left:
                    pass
                if kind == "mm":
                    project_out(0, range(2 * NPAIR))
                pe.wait_ge(y_ready, pair_no(kind, it) + 1)
                for c in range(2 * pairs_of(kind)):
                    q = len(pieces) + c
                    pe.wait_ge(piece_done, piece_no(kind, it, q) - 1)
                    for b in range(4):
                        mm = pe.transpose(banks[:, bank_of(kind, it, q), b * P:(b + 1) * P],
                                          y_of[c // 2][:, 4 * (c % 2) + b, :, :].rearrange("p h c -> p (h c)"), ident[:, :])
                    mm.then_inc(piece_ready, 1)

            def project_out(m, tiles):
                b = m % 2
                if tiles[0] == 0:
                    pe.wait_ge(yb_lo, m + 1)
                    if m >= 2:
                        pe.wait_ge(res_sum, m - 1)
                elif m == 0:
                    pe.wait_ge(my_lo, 2 * MPAIR)
                for j in tiles:
                    if m == 0:
                        pe.wait_ge(wo_lo, j + 1)
                    for l, r in ((0, 0), (0, 1), (1, 0)):
                        yt = y_hl[b][:, l, j, :] if j < 2 * NPAIR else mem_hl[:, l, j - 2 * NPAIR, m * P:(m + 1) * P]
                        for c in range(2):
                            mm = pe.matmul(banks[:, 2 * b + c, :], yt, wo_hl[j][:, r, c * CW:(c + 1) * CW],
                                           start=(j == 0 and (l, r) == (0, 0)), stop=(j == NT_OUT - 1 and l == 1))
                if tiles[-1] == NT_OUT - 1:
                    mm.then_inc(proj_out, 1)

            def transpose_x(c, k):
                g = c * KT + k
                if g >= 2:
                    pe.wait_ge(xT_lo, g - 1)
                for b in range(4):
                    mm = pe.transpose(banks[:, T_BANK + g % 2, b * P:(b + 1) * P], x_rows[4 * c + b][:, k * P:(k + 1) * P],
                                      ident[:, :])
                mm.then_inc(xT_ready, 1)

            def forget_logits():
                pe.wait_ge(wf_lo, 1)
                for c in range(2):
                    tok = slice(c * CW, (c + 1) * CW)
                    for k in range(KT):
                        f = slice(k * FH, (k + 1) * FH)
                        o = banks[0:FH, S_BANK + c, :]
                        pe.matmul(o, forget_hi[:, f], hT[:, 0, k, tok], start=(k == 0), stop=False)
                        pe.matmul(o, forget_hi[:, f], hT[:, 1, k, tok], start=False, stop=False)
                        mm = pe.matmul(o, forget_lo[:, f], hT[:, 0, k, tok], start=False, stop=(k == KT - 1))
                    mm.then_inc(f_logit, 1)

            pe.wait_ge(ident_done, 1)
            pe.wait_ge(x_scaled, 4)
            for k in range(KT):
                transpose_x(0, k)
            pe.wait_ge(xT_lo, KT)
            for q, (what, tile, c, _) in enumerate(FIRST_ORDER):
                if q >= 2:
                    pe.wait_ge(piece_done, q - 1)
                if q == 1:
                    pe.wait_ge(x_scaled, NB)
                if q == 2:
                    pe.wait_ge(xT_lo, 2 * KT)
                    forget_logits()
                if what == "VT":
                    transpose_values(c, PJ_BANK + q % 2)
                    continue
                for k, _ in enumerate(project(tile, tile % 2, c, PJ_BANK + q % 2)):
                    if q == 1:
                        transpose_x(1, k)
            head("sb", 0)
            with pe.Fori(0, NPAIR - 1) as it:
                phase("sb", it, ("fx", it))
                phase("fx", it, ("sb", it + 1))
            phase("sb", NPAIR - 1, ("last", NPAIR - 1))
            phase("last", NPAIR - 1, ("mm", 0))
            phase("mm", 0)
            project_out(1, range(2 * NPAIR))
            for m in range(NB):
                if m >= 2:
                    project_out(m, range(2 * NPAIR))
                project_out(m, range(2 * NPAIR, NT_OUT))

        @block.scalar
        def _(act):
            def split_hi(n, parity):
                act.wait_ge(w_in_dma, (n + 1) * 16)
                act.activation(w_parts[:, parity, 0, :], w_raw[:, :], ACT.Copy).then_inc(w_hi, 1)

            def evacuate(kind, it, piece, q_no, bank):
                what, tile, c, _ = piece
                act.wait_ge(piece_ready, q_no + 1)
                if what == "V":
                    return
                src = banks[:, bank, :]
                cols = slice(c * CW, (c + 1) * CW)
                if what == "Q":
                    q = q_of(target_of(kind))
                    act.activation(q[0:HD, 0, cols], src[0:HD], ACT.Copy, scale=SCALE)
                    ins = act.activation(q[HD:P, 1, cols], src[HD:P], ACT.Copy, scale=SCALE)
                elif what == "K":
                    k = k_of(target_of(kind))
                    act.activation(k[0:HD, 0, 0, cols], src[0:HD], ACT.Copy)
                    ins = act.activation(k[HD:P, 1, 0, cols], src[HD:P], ACT.Copy)
                elif what == "VT":
                    ins = act.activation(v_of(target_of(kind))[:, 4 * c:4 * c + 4, :, 0:HD],
                                         src.rearrange("p (b h c) -> p b h c", b=4, h=2), ACT.Copy)
                elif what in ("G0", "G1", "memG0", "memG1"):
                    if what in ("memG0", "memG1"):
                        act.wait_ge(y_out, 16 * (2 * NPAIR - 1 + int(what[-1])))
                    ins = act.activation(silu[:, int(what[-1]), cols], src, ACT.Sigmoid)
                elif what == "memT":
                    for i in range(2):
                        k = 2 * c + i
                        ins = act.activation(memT[:, 0, k, :], src[:, i * MEM:(i + 1) * MEM], ACT.Copy, scale=mem_g[:, k:k + 1])
                elif what == "memK":
                    act.activation(mem_k[0:HD, 2 * c, 0, :], src[0:HD, 0:MEM], ACT.Copy)
                    ins = act.activation(mem_k[HD:P, 2 * c + 1, 0, :], src[HD:P, 0:MEM], ACT.Copy)
                elif what == "memV":
                    for b in range(MB):
                        ins = act.activation(mem_v[:, b, 2 * c:2 * c + 2, 0:HD],
                                             src[:, b * P:(b + 1) * P].rearrange("p (h c) -> p h c", h=2), ACT.Copy)
                elif what in ("memQ0", "memQ1"):
                    h = 2 * int(what[-1])
                    act.activation(mem_q[0:HD, h, cols], src[0:HD], ACT.Copy, scale=SCALE)
                    ins = act.activation(mem_q[HD:P, h + 1, cols], src[HD:P], ACT.Copy, scale=SCALE)
                ins.then_inc(piece_hi, 1)

            def evacuate_and_split(kind, it, q):
                pieces = PIECES[kind]
                evacuate(kind, it, pieces[q], piece_no(kind, it, q), bank_of(kind, it, q))
                if closes_tile(pieces[q]):
                    n = tile_no(kind, it, pieces[q][1])
                    if kind in ("sb", "fx") or n + 2 < N_TILES:
                        split_hi(n + 2, tile_parity(kind, it, pieces[q][1]))

            def sigmoids(it, u):
                h, tb = head_block(u)
                if u >= RING:
                    act.wait_ge(t_ready, it * 48 + Causal.before(u - RING + 1))
                for i, (c0, c1) in enumerate(spans(Causal.width(u))):
                    g = Causal.before(u) + i
                    act.wait_ge(s_ready, chunk_no("sb", it, g) + 1)
                    src = banks[:, S_BANK + g % 3, 0:c1 - c0]
                    act.activation(work[:, u % RING, c0:c1], src, ACT.Sigmoid, scale=-1.0)
                    act.activation(work[:, RING + u % RING, c0:c1], src, ACT.Sigmoid).then_inc(sb_read, 1)

            def exponentials(kind, it, u):
                act.wait_ge(fx_max, unit_no(kind, it, u) + 1)
                h, tb = head_block(u, kind)
                p = work[:, u % RING, 0:geometry(kind).width(u)]
                if kind == "mm":
                    if u >= RING:
                        act.wait_ge(t_ready, group_no(kind, it, u - RING) + 1)
                    act.activation(p, banks[:, S_BANK + u % 3, 0:MEM], ACT.Exp, bias=npeak[:, u:u + 1],
                                   accum_out=rowsum[:, u:u + 1]).then_inc(fx_p, 1)
                else:
                    act.activation(p, p, ACT.Exp, bias=npeak[:, u:u + 1], accum_out=rowsum[:, u:u + 1]).then_inc(fx_p, 1)

            def upper_parts(kind, it, u):
                geo = geometry(kind)
                n_sb = geo.width(u) // P
                for i in range((n_sb + 3) // 4):
                    g = geo.before(u) + i
                    n = min(4, n_sb - 4 * i) * P
                    act.wait_ge(t_ready, group_no(kind, it, g) + 1)
                    if g >= 3:
                        act.wait_ge(pv_done, group_no(kind, it, g) - 2)
                    act.activation(pT[:, g % 3, 0, 0:n], banks[:, T_BANK + g % 2, 0:n],
                                   ACT.Copy).then_inc(t_hi, 1)

            def output_lo(kind, it, half):
                geo = geometry(kind)
                act.wait_ge(pv_done, group_no(kind, it, geo.before(4 * half + 4)))
                if half:
                    act.wait_ge(o_done, half_no(kind, it, half))
                act.activation(o_tmp[:, :, :], banks[:, O_BANK, :].rearrange("p (b c) -> p b c", b=4)[:, :, HD:P],
                               ACT.Copy).then_inc(o_lo, 1)

            def mem_norm(stage):
                if stage == 0:
                    act.wait_ge(mem_in, 16 * MB)
                    for b in range(MB):
                        act.activation(work[:, RING + 2, :], mem_rows[b], ACT.Square, accum_out=rs[:, 2, b:b + 1]).then_inc(mem_ssq, 1)
                        act.wait_ge(mem_ssq, b + 1)
                else:
                    act.wait_ge(mem_rstd, 1)
                    for b in range(MB):
                        act.activation(mem_rows[b], mem_rows[b], ACT.Copy, scale=rs[:, 1, b:b + 1]).then_inc(mem_scaled, 1)

            def w_out_hi(j):
                act.wait_ge(wo_in[j % 3], 16 * (j // 3 + 1))
                act.activation(wo_hl[j][:, 0, :], wo_raw[j % 3], ACT.Copy).then_inc(wo_hi, 1)

            def y_hi(m):
                act.wait_ge(yb_in[m % 2], 16 * (m // 2 + 1))
                if m >= 2:
                    act.wait_ge(proj_out, m - 1)
                act.activation(y_hl[m % 2][:, 0, :, :], y_raw[m % 2].rearrange("p (j t) -> p j t", j=2 * NPAIR),
                               ACT.Copy).then_inc(yb_hi, 1)

            def first_parts(kind, it, i):
                if kind == "sb":
                    if i < N_UNITS[kind]:
                        sigmoids(it, i)
                elif 0 <= i - EXP_LAG < N_UNITS[kind]:
                    exponentials(kind, it, i - EXP_LAG)

            def head(kind, it):
                for i in range(HEAD):
                    first_parts(kind, it, i)

            def phase(kind, it, following=None):
                pieces = PIECES[kind]
                issue, done, last = plan(kind)
                for i in range(HEAD, STEPS[kind]):
                    first_parts(kind, it, i)
                    if following and early_row(kind, i) is not None:
                        if early_row(kind, i) == (0 if following[0] == "sb" else EXP_LAG):
                            act.wait_ge(t_ready, chunk_no(*following, 0))
                        first_parts(*following, early_row(kind, i))
                    if kind == "last" and MEM_STEP <= i < MEM_STEP + 2:
                        mem_norm(i - MEM_STEP)
                    if kind == "mm" and i in WO_STEP:
                        w_out_hi(WO_STEP[i])
                    if kind == "mm" and i in Y_STEP:
                        y_hi(Y_STEP[i])
                    for q in done[i]:
                        evacuate_and_split(kind, it, q)
                    if T_LAG <= i < N_UNITS[kind] + T_LAG:
                        upper_parts(kind, it, i - T_LAG)
                    if PV_LAG[kind] <= i and (i - PV_LAG[kind]) % 4 == 3:
                        output_lo(kind, it, (i - PV_LAG[kind]) // 4)
                for q in last:
                    evacuate_and_split(kind, it, q)

            def square(b):
                act.wait_ge(x_in[b], 16)
                if b:
                    act.wait_ge(x_ssq, b)
                act.activation(y_flat, x_rows[b], ACT.Square, accum_out=ssq[:, 0, b, 0:1]).then_inc(x_ssq, 1)

            def x_hi(c, k):
                act.wait_ge(xT_ready, c * KT + k + 1)
                act.activation(hT[:, 0, k, c * CW:(c + 1) * CW], banks[:, T_BANK + k % 2, :], ACT.Copy,
                               scale=in_g[:, k:k + 1]).then_inc(xT_hi, 1)

            for b in range(4):
                square(b)
            split_hi(0, 0)
            act.wait_ge(consts_in, 64)
            for k in range(KT):
                x_hi(0, k)
                if k % 2:
                    square(4 + k // 2)
            act.wait_ge(wf_in, 16)
            act.activation(forget_hi, diag[:, 0, 0:KT * FH], ACT.Copy).then_inc(wf_hi, 1)
            split_hi(1, 1)
            for q, piece in enumerate(FIRST_ORDER):
                evacuate("fx", 0, piece, q, PJ_BANK + q % 2)
                if q == 0:
                    for k in range(KT):
                        x_hi(1, k)
                if q == 1:
                    act.wait_ge(f_abs, 1)
                    act.activation(f_a, f_a, ACT.Exp, scale=-1.0).then_inc(f_exp, 1)
                    act.wait_ge(f_exp, 1)
                    act.activation(f_a, f_a, ACT.Ln, bias=1.0).then_inc(f_ln, 1)
                if closes_tile(piece):
                    split_hi(piece[1] + 2, piece[1] % 2)
            head("sb", 0)
            with act.Fori(0, NPAIR - 1) as it:
                phase("sb", it, ("fx", it))
                phase("fx", it, ("sb", it + 1))
            phase("sb", NPAIR - 1, ("last", NPAIR - 1))
            phase("last", NPAIR - 1, ("mm", 0))
            phase("mm", 0)
            for c in range(2 * MPAIR):
                act.wait_ge(piece_done, piece_no("mm", 0, len(PIECES["mm"]) + c) + 1)
                cols = slice(c % 2 * CW, (c % 2 + 1) * CW)
                act.activation(mem_hl[:, 0, c // 2, cols], silu[:, c // 2, cols], ACT.Copy).then_inc(my_hi, 1)
            for m in range(NB):
                if m + 2 < NB:
                    y_hi(m + 2)
                act.wait_ge(res_sum, m + 1)
                if m:
                    act.wait_ge(res_ssq, m)
                act.activation(squares, res[m % RING], ACT.Square, accum_out=rs[:, 2, 0:1]).then_inc(res_ssq, 1)

        @block.gpsimd
        def _(pool):
            fill_one, fill_zero, fill_lowest = pool.to_reg(1.0), pool.to_reg(0.0), pool.to_reg(LOWEST)

            def split_lo(n, parity):
                pool.wait_ge(w_hi, n + 1)
                pool.tensor_tensor(w_parts[:, parity, 1, :], w_raw[:, :], w_parts[:, parity, 0, :].bitcast(F32),
                                   ALU.subtract).then_inc(w_lo, 1)

            def masks(it, u):
                h, tb = head_block(u)
                wait_alone(pool, sb_read, it * 24 + Causal.before(u + 1))
                blk = slice(tb * P, (tb + 1) * P)
                f, b = work[:, u % RING, blk], work[:, RING + u % RING, blk]
                pool.affine_select(out=f, in_=f, compare_op=ALU.is_gt, fill=fill_one, base=0, pattern=[[-1, P]],
                                   channel_multiplier=1).then_inc(fail_masked, 1)
                pool.affine_select(out=b, in_=b, compare_op=ALU.is_gt, fill=fill_zero, base=0, pattern=[[-1, P]],
                                   channel_multiplier=1).then_inc(beta_masked, 1)

            def diagonal(kind, it, u):
                h, tb = head_block(u, kind)
                if u >= 2:
                    wait_alone(pool, fx_read, it * 24 + Causal.before(u - 1))
                pool.affine_select(out=diag[:, u % 2, :], in_=negL[:, h, tb * P:(tb + 1) * P], compare_op=ALU.is_ge,
                                   fill=fill_lowest, base=0, pattern=[[-1, P]], channel_multiplier=1).then_inc(diag_ready, 1)

            def maybe_split(kind, it, q):
                pieces = PIECES[kind]
                if closes_tile(pieces[q]):
                    n = tile_no(kind, it, pieces[q][1])
                    if kind in ("sb", "fx") or n + 2 < N_TILES:
                        split_lo(n + 2, tile_parity(kind, it, pieces[q][1]))

            def head(kind, it):
                for i in range(HEAD):
                    mask(kind, it, i)

            def mask(kind, it, i):
                if kind in ("fx", "last") and i == 0:
                    wait_alone(pool, negL_in, it * 32 + 32)
                if kind == "sb" and i < UNITS:
                    masks(it, i)
                elif kind in ("fx", "last") and i < UNITS:
                    diagonal(kind, it, i)

            def phase(kind, it, following=None):
                issue, done, last = plan(kind)
                for i in range(HEAD, STEPS[kind]):
                    mask(kind, it, i)
                    if following and early_row(kind, i) is not None:
                        mask(*following, early_row(kind, i))
                    for q in done[i]:
                        maybe_split(kind, it, q)
                for q in last:
                    maybe_split(kind, it, q)

            pool.memset(ident[:, :], 0.0).then_inc(ident_zero, 1)
            pool.wait_ge(ident_zero, 1)
            pool.affine_select(out=ident[:, :], in_=ident[:, :], compare_op=ALU.not_equal, fill=1.0, base=0,
                               pattern=[[-1, P]], channel_multiplier=1).then_inc(ident_done, 1)
            split_lo(0, 0)
            pool.wait_ge(wf_hi, 1)
            pool.tensor_tensor(forget_lo, diag[:, 0, 0:KT * FH], forget_hi.bitcast(F32), ALU.subtract).then_inc(wf_lo, 1)
            split_lo(1, 1)
            for t in range(FIRST_TILES):
                split_lo(t + 2, t % 2)
            head("sb", 0)
            with pool.Fori(0, NPAIR - 1) as it:
                phase("sb", it, ("fx", it))
                phase("fx", it, ("sb", it + 1))
            phase("sb", NPAIR - 1, ("last", NPAIR - 1))
            phase("last", NPAIR - 1, ("mm", 0))
            phase("mm", 0)
            for j in range(NT_OUT):
                pool.wait_ge(wo_hi, j + 1)
                pool.tensor_tensor(wo_hl[j][:, 1, :], wo_raw[j % 3], wo_hl[j][:, 0, :].bitcast(F32), ALU.subtract).then_inc(wo_lo, 1)

        @block.vector
        def _(dve):
            steps = {"base": 0, "n": 0}

            def link(ins):
                steps["n"] += 1
                ins.then_inc(dve_step, 1)
                dve.wait_ge(dve_step, steps["base"] + steps["n"])

            def rsqrt(v, n, mean, last=None):
                r, half, t = rs[:, 0, 0:n], rs[:, 2, 0:n], rs[:, 1, 0:n]
                link(dve.tensor_scalar(half, v, 1.0 / mean, EPS, ALU.mult, ALU.add))
                link(dve.tensor_scalar(t.bitcast(I32), half.bitcast(I32), 1, None, ALU.logical_shift_right))
                link(dve.tensor_scalar(r.bitcast(I32), t.bitcast(I32), -1.0, float(0x5F3759DF), ALU.mult, ALU.add))
                link(dve.tensor_scalar(half, half, -0.5, None, ALU.mult))
                for _ in range(3):
                    link(dve.tensor_tensor(t, r, r, ALU.mult))
                    link(dve.tensor_tensor(t, t, half, ALU.mult))
                    link(dve.scalar_tensor_tensor(out=r, in0=t, scalar=1.5, in1=r, op0=ALU.add, op1=ALU.mult))

            def evacuate(kind, piece, number, n_hi, bank, sent=None):
                what, tile, c, _ = piece
                src = banks[:, bank, :]
                if what == "V":
                    dve.wait_ge(piece_ready, number + 1)
                    if sent is not None:
                        dve.wait_ge(y_out, sent)
                    dve.tensor_copy(v_raw(c), src).then_inc(piece_done, 1)
                    return
                dve.wait_ge(piece_hi, n_hi + 1)
                cols = slice(c * CW, (c + 1) * CW)

                def scaled(dst, s, hi):
                    return dve.scalar_tensor_tensor(out=dst, in0=s, scalar=SCALE, in1=hi.bitcast(F32), op0=ALU.mult, op1=ALU.subtract)

                if what == "Q":
                    q = q_of(target_of(kind))
                    scaled(q[HD:P, 0, cols], src[0:HD], q[0:HD, 0, cols])
                    ins = scaled(q[0:HD, 1, cols], src[HD:P], q[HD:P, 1, cols])
                elif what == "K":
                    k = k_of(target_of(kind))
                    dve.tensor_tensor(k[0:HD, 0, 1, cols], src[0:HD], k[0:HD, 0, 0, cols].bitcast(F32), ALU.subtract)
                    ins = dve.tensor_tensor(k[HD:P, 1, 1, cols], src[HD:P], k[HD:P, 1, 0, cols].bitcast(F32), ALU.subtract)
                elif what == "VT":
                    v = v_of(target_of(kind))[:, 4 * c:4 * c + 4, :, :]
                    ins = dve.tensor_tensor(v[:, :, :, HD:P], src.rearrange("p (b h c) -> p b h c", b=4, h=2),
                                            v[:, :, :, 0:HD].bitcast(F32), ALU.subtract)
                elif what in ("G0", "G1", "memG0", "memG1"):
                    g = silu[:, int(what[-1]), cols]
                    ins = dve.tensor_tensor(g, src, g, ALU.mult)
                elif what == "memT":
                    for i in range(2):
                        k = 2 * c + i
                        ins = dve.scalar_tensor_tensor(out=memT[:, 1, k, :], in0=src[:, i * MEM:(i + 1) * MEM],
                                                       scalar=mem_g[:, k:k + 1], in1=memT[:, 0, k, :].bitcast(F32),
                                                       op0=ALU.mult, op1=ALU.subtract)
                elif what == "memK":
                    dve.tensor_tensor(mem_k[0:HD, 2 * c, 1, :], src[0:HD, 0:MEM], mem_k[0:HD, 2 * c, 0, :].bitcast(F32), ALU.subtract)
                    ins = dve.tensor_tensor(mem_k[HD:P, 2 * c + 1, 1, :], src[HD:P, 0:MEM],
                                            mem_k[HD:P, 2 * c + 1, 0, :].bitcast(F32), ALU.subtract)
                elif what == "memV":
                    for b in range(MB):
                        v = mem_v[:, b, 2 * c:2 * c + 2, :]
                        ins = dve.tensor_tensor(v[:, :, HD:P], src[:, b * P:(b + 1) * P].rearrange("p (h c) -> p h c", h=2),
                                                v[:, :, 0:HD].bitcast(F32), ALU.subtract)
                elif what in ("memQ0", "memQ1"):
                    h = 2 * int(what[-1])
                    scaled(mem_q[HD:P, h, cols], src[0:HD], mem_q[0:HD, h, cols])
                    ins = scaled(mem_q[0:HD, h + 1, cols], src[HD:P], mem_q[HD:P, h + 1, cols])
                ins.then_inc(piece_done, 1)

            def stick(kind, it, u):
                w = Causal.width(u)
                f, b = work[:, u % RING, :], work[:, RING + u % RING, :]
                dve.wait_ge(fail_masked, it * UNITS + (u + 1))
                left = f[:, w - 1:0:-1]
                dve.tensor_tensor_scan(left, left, left, 1.0, ALU.mult, ALU.bypass).then_inc(scanned, 1)
                dve.wait_ge(beta_masked, it * UNITS + (u + 1))
                dve.wait_ge(scanned, it * UNITS + (u + 1))
                dve.tensor_tensor(b[:, 0:w - 1], b[:, 0:w - 1], f[:, 1:w], ALU.mult).then_inc(sb_p, 1)

            def logits(kind, it, u):
                h, tb = head_block(u, kind)
                if u >= RING:
                    dve.wait_ge(t_ready, group_no(kind, it, Causal.before(u - RING + 1)))
                dve.wait_ge(diag_ready, it * UNITS + (u + 1))
                start, n = LOWEST, 4 * (u % RING)
                for i, (c0, c1) in enumerate(spans(Causal.width(u))):
                    g = Causal.before(u) + i
                    wait_alone(dve, s_ready, chunk_no(kind, it, g) + 1)
                    cuts = [(a, b) for a, b in ((c0, min(c1, tb * P)), (max(c0, tb * P), c1)) if a < b]
                    for a, b in cuts:
                        bias = diag[:, u % 2, :] if a == tb * P else negL[:, h, a:b]
                        ins = dve.tensor_tensor_reduce(out=work[:, u % RING, a:b], in0=banks[:, S_BANK + g % 3, a - c0:b - c0],
                                                       in1=bias, scale=1.0, scalar=start, op0=ALU.add, op1=ALU.max,
                                                       accum_out=peak[:, n:n + 1])
                        start, n = peak[:, n:n + 1], n + 1
                        if b == c1:
                            ins.then_inc(fx_read, 1)
                            wait_alone(dve, fx_read, it * 24 + (g + 1))
                        else:
                            steps["n"] += 1
                            ins.then_inc(dve_step, 1)
                            wait_alone(dve, dve_step, steps["base"] + steps["n"])
                dve.tensor_scalar(npeak[:, u:u + 1], start, -1.0, None, ALU.mult).then_inc(fx_max, 1)

            def mem_max(kind, it, u):
                dve.wait_ge(s_ready, chunk_no(kind, it, u) + 1)
                top = peak[:, 4 * (u % RING):4 * (u % RING) + 1]
                link(dve.reduce_max(top, banks[:, S_BANK + u % 3, 0:MEM], AX_X))
                dve.tensor_scalar(npeak[:, u:u + 1], top, -1.0, None, ALU.mult).then_inc(fx_max, 1)

            def rows(kind, it, u):
                (stick if kind == "sb" else mem_max if kind == "mm" else logits)(kind, it, u)

            def head(kind, it):
                for u in range(HEAD):
                    rows(kind, it, u)

            def phase(kind, it, following=None):
                pieces = PIECES[kind]
                issue, done, last = plan(kind)
                geo = geometry(kind)

                def piece(q):
                    evacuate(kind, pieces[q], piece_no(kind, it, q), hi_no(kind, it, q), bank_of(kind, it, q),
                             it * 32 + 16 if kind == "fx" else None)

                def lower_parts(u):
                    n_sb = geo.width(u) // P
                    for i in range((n_sb + 3) // 4):
                        g = geo.before(u) + i
                        n = min(4, n_sb - 4 * i) * P
                        dve.wait_ge(t_hi, group_no(kind, it, g) + 1)
                        part = pT[:, g % 3, :, 0:n]
                        dve.tensor_tensor(part[:, 1, :], banks[:, T_BANK + g % 2, 0:n], part[:, 0, :].bitcast(F32),
                                          ALU.subtract).then_inc(t_lo, 1)

                def output(half):
                    pair, bank = half // 4, banks[:, O_BANK, :].rearrange("p (b c) -> p b c", b=4)
                    if kind == "mm":
                        blocks = [(slice(0, 4), 4 * (half % 2), 4, half // 2 % 2)]
                    else:
                        blocks = [(slice(u % 2, 4, 2), head_block(u)[1], 2, head_block(u)[0]) for u in (4 * half, 4 * half + 1)]
                    places = [(where, y_of[pair][:, b0:b0 + n, h, :], ssq[:, pair, b0:b0 + n, h], n) for where, b0, n, h in blocks]
                    dve.wait_ge(o_lo, half_no(kind, it, half) + 1)
                    for where, o, _, n in places:
                        ins = dve.tensor_tensor(o, bank[:, where, 0:HD], o_tmp[:, where, :], ALU.add)
                    ins.then_inc(o_read, 1)
                    dve.wait_ge(o_read, half_no(kind, it, half) + 1)
                    if kind != "sb":
                        link(dve.reciprocal(rinv[:, :], rowsum[:, 4 * half:4 * half + 4]))
                        for where, o, _, n in places:
                            ins = dve.tensor_tensor(o, o, rinv[:, where].unsqueeze(2).broadcast_to((P, n, HD)), ALU.mult)
                        link(ins)
                    for where, o, _, n in places:
                        ins = dve.tensor_tensor(o_tmp[:, where, :], o, o, ALU.mult)
                    link(ins)
                    for where, _, sums, n in places:
                        ins = dve.reduce_sum(sums, o_tmp[:, where, :], AX_X)
                    ins.then_inc(o_done, 1)

                for i in range(HEAD, STEPS[kind]):
                    early = early_row(kind, i) if following else None
                    if i < N_UNITS[kind] and kind != "sb":
                        rows(kind, it, i)
                    if early is not None and following[0] != "sb":
                        if early == 0 and following[0] != "mm":
                            dve.wait_ge(t_ready, chunk_no(*following, 0))
                        rows(*following, early)
                    if kind == "last" and i == MEM_STEP + 1:
                        dve.wait_ge(mem_ssq, MB)
                        rsqrt(rs[:, 2, 0:MB], MB, D)
                        dve.tensor_copy(rs[:, 1, 0:MB], rs[:, 0, 0:MB]).then_inc(mem_rstd, 1)
                    for q in done[i]:
                        piece(q)
                    if T_LAG <= i < N_UNITS[kind] + T_LAG:
                        lower_parts(i - T_LAG)
                    if i < N_UNITS[kind] and kind == "sb":
                        rows(kind, it, i)
                    if early is not None and following[0] == "sb":
                        rows(*following, early)
                    if kind == "mm" and i in Y_STEP:
                        y_lo(Y_STEP[i])
                    if PV_LAG[kind] <= i and (i - PV_LAG[kind]) % 4 == 3:
                        output((i - PV_LAG[kind]) // 4)
                n_pairs = pairs_of(kind)
                dve.wait_ge(o_done, half_no(kind, it, N_UNITS[kind] // 4 - 1) + 1)
                rsqrt(ssq[:, 0:n_pairs, :, :].rearrange("p a b h -> p (a b h)"), UNITS * n_pairs, HD)
                for pair in range(n_pairs):
                    yv = y_of[pair].rearrange("p b h c -> p (b h) c")
                    r = rs[:, 0, UNITS * pair:UNITS * (pair + 1)]
                    ins = dve.tensor_tensor(yv, yv, r.unsqueeze(2).broadcast_to((P, UNITS, HD)), ALU.mult)
                ins.then_inc(y_ready, 1)
                for q in last:
                    piece(q)
                for c in range(2 * n_pairs):
                    q = len(pieces) + c
                    dve.wait_ge(piece_ready, piece_no(kind, it, q) + 1)
                    g = silu[:, side_of(kind, c // 2), c % 2 * CW:(c % 2 + 1) * CW]
                    t = out_tile(kind, it, c // 2)
                    dve.scalar_tensor_tensor(out=g, in0=banks[:, bank_of(kind, it, q), :], scalar=out_g[:, bass.ds(t, 1)], in1=g,
                                             op0=ALU.mult, op1=ALU.mult).then_inc(piece_done, 1)

            def y_lo(m):
                dve.wait_ge(yb_hi, m + 1)
                dve.tensor_tensor(y_hl[m % 2][:, 1, :, :], y_raw[m % 2].rearrange("p (j t) -> p j t", j=2 * NPAIR),
                                  y_hl[m % 2][:, 0, :, :].bitcast(F32), ALU.subtract).then_inc(yb_lo, 1)

            def scale_x(c):
                dve.wait_ge(x_ssq, 4 * (c + 1))
                if c:
                    dve.wait_ge(x_scaled, 4)
                rsqrt(ssq[:, 0, 4 * c:4 * c + 4, 0], 4, D)
                for b in range(4):
                    row = x_rows[4 * c + b]
                    dve.tensor_scalar(row, row, rs[:, 0, b:b + 1], None, ALU.mult).then_inc(x_scaled, 1)

            def x_lo(c, k):
                cols = slice(c * CW, (c + 1) * CW)
                dve.wait_ge(xT_hi, c * KT + k + 1)
                dve.scalar_tensor_tensor(out=hT[:, 1, k, cols], in0=banks[:, T_BANK + k % 2, :], scalar=in_g[:, k:k + 1],
                                         in1=hT[:, 0, k, cols].bitcast(F32), op0=ALU.mult, op1=ALU.subtract).then_inc(xT_lo, 1)

            def forget_gates():
                dve.wait_ge(f_logit, 2)
                for c in range(2):
                    link(dve.tensor_scalar(f_u[:, c * CW:(c + 1) * CW], banks[0:FH, S_BANK + c, :], b_f[:, 0:1], None, ALU.add))
                dve.scalar_tensor_tensor(out=f_a, in0=f_u, scalar=-1.0, in1=f_u, op0=ALU.mult, op1=ALU.max).then_inc(f_abs, 1)
                link(dve.tensor_scalar(f_m, f_u, -1.0, 0.0, ALU.mult, ALU.max))
                link(dve.memset(f_one, 1.0))
                dve.wait_ge(f_ln, 1)
                link(dve.tensor_tensor(f_m, f_m, f_a, ALU.add))
                dve.tensor_tensor_scan(f_m, f_one, f_m, 0.0, ALU.mult, ALU.add).then_inc(f_scan, 1)

            scale_x(0)
            dve.wait_ge(consts_in, 64)
            for k in range(KT):
                x_lo(0, k)
            scale_x(1)
            for q, piece in enumerate(FIRST_ORDER):
                evacuate("fx", piece, q, sum(p[0] != "V" for p in FIRST_ORDER[:q]), PJ_BANK + q % 2)
                if q == 0:
                    for k in range(KT):
                        x_lo(1, k)
                if q == 1:
                    forget_gates()
            before_loop = steps["n"]
            head("sb", 0)
            with dve.Fori(0, NPAIR - 1) as it:
                steps["base"], steps["n"] = it * TURN_STEPS + before_loop, 0
                phase("sb", it, ("fx", it))
                phase("fx", it, ("sb", it + 1))
                assert steps["n"] == TURN_STEPS, steps["n"]
            steps["base"], steps["n"] = before_loop + (NPAIR - 1) * TURN_STEPS, 0
            phase("sb", NPAIR - 1, ("last", NPAIR - 1))
            phase("last", NPAIR - 1, ("mm", 0))
            phase("mm", 0)
            for c in range(2 * MPAIR):
                dve.wait_ge(my_hi, c + 1)
                cols = slice(c % 2 * CW, (c % 2 + 1) * CW)
                dve.tensor_tensor(mem_hl[:, 1, c // 2, cols], silu[:, c // 2, cols], mem_hl[:, 0, c // 2, cols].bitcast(F32),
                                  ALU.subtract).then_inc(my_lo, 1)
            dve.wait_ge(fin_in, 16)
            for m in range(NB):
                b = m % 2
                r = res[m % RING]
                dve.wait_ge(proj_out, m + 1)
                dve.wait_ge(xb_in[m % RING], 16 * (m // RING + 1))
                dve.tensor_tensor(r, banks[:, 2 * b:2 * b + 2, :].rearrange("p b c -> p (b c)"), r, ALU.add).then_inc(res_sum, 1)
                if m + 2 < NB:
                    y_lo(m + 2)
                dve.wait_ge(res_ssq, m + 1)
                rsqrt(rs[:, 2, 0:1], 1, D)
                dve.scalar_tensor_tensor(out=r, in0=r, scalar=rs[:, 0, 0:1], in1=final_g, op0=ALU.mult,
                                         op1=ALU.mult).then_inc(res_done, 1)


def kernel(x, mem, norm_w, w_in, b_forget, mem_norm_w, w_mem_kv, out_norm_w, w_out, final_norm_w):
    import numpy as np
    import concourse.bacc as bacc
    from concourse import mybir as mb
    from concourse.bass_utils import run_bass_kernel_spmd

    def tiles(w, starts):
        w = np.asarray(w)
        return [w[:, s:s + P].reshape(KT, P, P).transpose(1, 0, 2).reshape(P, KT * P) for s in starts]

    w = np.asarray(w_in)[0]
    sbw, gate0, mq0, f0 = 512, 3336, 3080, 3072
    qkv = lambda base, pair: [base + i * sbw + pair * P for i in (1, 0, 2)]
    order = []
    for it in range(NPAIR):
        if it == 0:
            order += qkv(0, 0)
        order += qkv(3 * sbw, it) + [gate0 + it * P, gate0 + (NPAIR + it) * P]
        if it < NPAIR - 1:
            order += qkv(0, it + 1)
    w_tiles = tiles(w, order) + tiles(np.asarray(w_mem_kv)[0], [0, P, 2 * P, 3 * P])
    w_tiles += tiles(w, [mq0, mq0 + P, gate0 + 2 * NPAIR * P, gate0 + (2 * NPAIR + 1) * P])
    w_forget = w[:, f0:f0 + FH].reshape(KT, P, FH).transpose(1, 0, 2).reshape(P, KT * FH)
    arrays = {
        "in_x": np.asarray(x), "in_mem": np.asarray(mem), "in_w_tiles": np.stack(w_tiles), "in_w_forget": w_forget,
        "in_w_out": np.asarray(w_out)[0], "in_norm_w": np.asarray(norm_w).reshape(KT, P).T,
        "in_mem_norm_w": np.asarray(mem_norm_w).reshape(KT, P).T, "in_out_norm_w": np.asarray(out_norm_w).reshape(NT_OUT, P).T,
        "in_b_forget": np.asarray(b_forget).reshape(FH, 1), "in_final_norm_w": np.asarray(final_norm_w).reshape(1, D),
    }
    arrays = {k: np.ascontiguousarray(v) for k, v in arrays.items()}
    nc = bacc.Bacc("TRN2", target_bir_lowering=False, num_devices=1)
    args = [nc.dram_tensor(k, v.shape, mb.dt.from_np(v.dtype), kind="ExternalInput").ap() for k, v in arrays.items()]
    args.append(nc.dram_tensor("out_y", (1, S, D), F32, kind="ExternalOutput").ap())
    hybrid_layer(nc, *args)
    r = run_bass_kernel_spmd(nc, [arrays], core_ids=[0])
    return r.results[0]["out_y"]
```
